# Optimizing a Trainium2 kernel written in Bass

```python
import jax, jax.numpy as jnp
from jax import lax
import numpy as np

D_MODEL = 2048
BATCH = 1
SEQ = 256
DEPTH = 1
DEC_BATCH = 8
DEC_SEQ = 16
PAST_LEN = 256

CHUNK = 64
SWA_WIDTH = D_MODEL // 2
GLA_WIDTH = D_MODEL - SWA_WIDTH
SWA_HEAD_DIM = 64
SWA_HEADS = SWA_WIDTH // SWA_HEAD_DIM
SWA_KV_HEADS = max(1, SWA_HEADS // 8)
SWA_GROUP = SWA_HEADS // SWA_KV_HEADS
WINDOW = 128
WINDOW_CHUNKS = WINDOW // CHUNK
BAND = (WINDOW_CHUNKS + 1) * CHUNK
GLA_HEADS = 4
GLA_DV = GLA_WIDTH // GLA_HEADS
GLA_DK = GLA_DV // 2
GLA_GATE_RANK = 16
GLA_GATE_NORM = 16.0
GLA_BLOCK = 16
N_GROUPS = 4
EXPERTS_PER_GROUP = 8
N_EXPERTS = N_GROUPS * EXPERTS_PER_GROUP
TOP_K = 2
EXPERT_HIDDEN = D_MODEL // 4
MOE_BLOCK = 128
N_MOD = 6
EPS = 1e-6
NEG_INF = -1e30

IN_SIZES = (SWA_HEADS * SWA_HEAD_DIM, SWA_KV_HEADS * SWA_HEAD_DIM, SWA_KV_HEADS * SWA_HEAD_DIM,
            GLA_HEADS * GLA_DK, GLA_HEADS * GLA_DK, GLA_HEADS * GLA_DV, GLA_HEADS * GLA_DV,
            GLA_GATE_RANK)
D_IN = sum(IN_SIZES)
SPLIT_POINTS = tuple(int(s) for s in np.cumsum(IN_SIZES)[:-1])

kernel_name = 'hymba_swa_gla_hmoe_stream_step'

def rmsnorm(x, g):
    xf = x.astype(jnp.float32)
    y = xf * lax.rsqrt(jnp.mean(xf * xf, axis=-1, keepdims=True) + EPS)
    return y.astype(x.dtype) * g

def adaln(c, w_ada, b_ada):
    mod = jax.nn.silu(c) @ w_ada + b_ada
    return jnp.split(mod[:, None, :], N_MOD, axis=-1)

def modulate(h, shift, scale):
    return h * (1 + scale) + shift

def project_inputs(h, w_in, w_gate_up, b_gate):
    B, T, _ = h.shape
    qa, ka, va, qb, kb, vb, rb, ab = jnp.split(h @ w_in, SPLIT_POINTS, axis=-1)
    qa = qa.reshape(B, T, SWA_KV_HEADS, SWA_GROUP, SWA_HEAD_DIM)
    ka = ka.reshape(B, T, SWA_KV_HEADS, SWA_HEAD_DIM)
    va = va.reshape(B, T, SWA_KV_HEADS, SWA_HEAD_DIM)
    qb = qb.reshape(B, T, GLA_HEADS, GLA_DK) * (GLA_DK ** -0.5)
    kb = kb.reshape(B, T, GLA_HEADS, GLA_DK)
    vb = vb.reshape(B, T, GLA_HEADS, GLA_DV)
    lg = jax.nn.log_sigmoid((ab @ w_gate_up + b_gate).astype(jnp.float32)) / GLA_GATE_NORM
    lg = lg.reshape(B, T, GLA_HEADS, GLA_DK)
    return qa, ka, va, qb, kb, vb, rb, lg

def softmax_with_sink(s, sink):
    sink = jnp.broadcast_to(sink, s.shape[:-1] + (1,))
    return jax.nn.softmax(jnp.concatenate([s, sink], axis=-1), axis=-1)[..., :-1]

def swa_prompt(q, k, v, sinks):
    B, T = k.shape[:2]
    nc = T // CHUNK

    def band(a):
        pad = jnp.zeros((B, WINDOW) + a.shape[2:], a.dtype)
        ac = jnp.concatenate([pad, a], axis=1).reshape(B, nc + WINDOW_CHUNKS, CHUNK, *a.shape[2:])
        return jnp.concatenate([ac[:, i:i + nc] for i in range(WINDOW_CHUNKS + 1)], axis=2)

    kband, vband = band(k), band(v)
    qc = q.reshape(B, nc, CHUNK, SWA_KV_HEADS, SWA_GROUP, SWA_HEAD_DIM)
    s = jnp.einsum('bncjgd,bnmjd->bnjgcm', qc, kband).astype(jnp.float32) * (SWA_HEAD_DIM ** -0.5)
    key_chunk = jnp.arange(nc)[:, None] - WINDOW_CHUNKS + jnp.arange(BAND)[None, :] // CHUNK
    s = jnp.where((key_chunk >= 0)[None, :, None, None, None, :], s, NEG_INF)
    sink = sinks.astype(jnp.float32).reshape(SWA_KV_HEADS, SWA_GROUP)[None, None, :, :, None, None]
    p = softmax_with_sink(s, sink)
    o = jnp.einsum('bnjgcm,bnmjd->bncjgd', p.astype(v.dtype), vband)
    return o.reshape(B, T, SWA_WIDTH)

def swa_sample(q, k_new, v_new, k_past, v_past, sinks):
    B, T = k_new.shape[:2]
    k = jnp.concatenate([k_past.astype(k_new.dtype), k_new], axis=1)
    v = jnp.concatenate([v_past.astype(v_new.dtype), v_new], axis=1)
    s = jnp.einsum('btjgd,bsjd->bjgts', q, k).astype(jnp.float32) * (SWA_HEAD_DIM ** -0.5)
    sink = sinks.astype(jnp.float32).reshape(SWA_KV_HEADS, SWA_GROUP)[None, :, :, None, None]
    p = softmax_with_sink(s, sink)
    o = jnp.einsum('bjgts,bsjd->btjgd', p.astype(v.dtype), v)
    return o.reshape(B, T, SWA_WIDTH)

def gla_block(s, q, k, v, lg):
    q, k, v = q.astype(jnp.float32), k.astype(jnp.float32), v.astype(jnp.float32)
    L = q.shape[1]
    b = jnp.cumsum(lg, axis=1)
    qd = q * jnp.exp(b)
    kd = k * jnp.exp(-b)
    causal = jnp.tril(jnp.ones((L, L), bool))
    a = jnp.where(causal, jnp.einsum('blhk,bshk->bhls', qd, kd), 0.0)
    o = jnp.einsum('blhk,bhkv->blhv', qd, s) + jnp.einsum('bhls,bshv->blhv', a, v)
    b_last = b[:, -1:]
    s_new = (jnp.exp(b_last[:, 0])[..., None] * s
             + jnp.einsum('bshk,bshv->bhkv', k * jnp.exp(b_last - b), v))
    return s_new, o

def gla_prompt(q, k, v, lg):
    B, T = q.shape[:2]
    nb = T // GLA_BLOCK

    def blocks(a):
        return a.astype(jnp.float32).reshape(B, nb, GLA_BLOCK, *a.shape[2:]).swapaxes(0, 1)

    s0 = jnp.zeros((B, GLA_HEADS, GLA_DK, GLA_DV), jnp.float32)
    s_fin, o = lax.scan(lambda s, blk: gla_block(s, *blk), s0,
                        (blocks(q), blocks(k), blocks(v), blocks(lg)))
    return s_fin, o.swapaxes(0, 1).reshape(B, T, GLA_HEADS, GLA_DV)

def mixer_output(oa, ob, rb, g_head, w_out):
    B, T, _ = oa.shape
    ob = rmsnorm(ob.astype(oa.dtype), g_head).reshape(B, T, GLA_WIDTH) * jax.nn.silu(rb)
    return jnp.concatenate([oa, ob], axis=-1) @ w_out

def expert_dispatch(x2, e_idx, gates, w_eg, w_eu, w_ed):
    N, D = x2.shape
    A = N * TOP_K
    flat_e = e_idx.reshape(-1)
    flat_w = gates.reshape(-1)
    flat_tok = jnp.arange(A, dtype=jnp.int32) // TOP_K
    order = jnp.argsort(flat_e)
    se = flat_e[order]
    counts = jnp.bincount(flat_e, length=N_EXPERTS)
    starts = jnp.cumsum(counts) - counts
    padded = (counts + MOE_BLOCK - 1) // MOE_BLOCK * MOE_BLOCK
    pend = jnp.cumsum(padded)
    pstart = pend - padded
    dest = pstart[se] + jnp.arange(A) - starts[se]
    n_blocks = -(-(A + N_EXPERTS * (MOE_BLOCK - 1)) // MOE_BLOCK)
    n_slots = n_blocks * MOE_BLOCK
    slot_tok = jnp.zeros((n_slots,), jnp.int32).at[dest].set(flat_tok[order])
    slot_w = jnp.zeros((n_slots,), x2.dtype).at[dest].set(flat_w[order].astype(x2.dtype))
    block_e = jnp.minimum(jnp.searchsorted(pend, jnp.arange(n_blocks) * MOE_BLOCK, side='right'),
                          N_EXPERTS - 1)
    xb = x2[slot_tok].reshape(n_blocks, MOE_BLOCK, D)

    def expert_block(args):
        xblk, e = args
        return (jax.nn.silu(xblk @ w_eg[e]) * (xblk @ w_eu[e])) @ w_ed[e]

    yb = lax.map(expert_block, (xb, block_e))
    return jax.ops.segment_sum(yb.reshape(n_slots, D) * slot_w[:, None], slot_tok, num_segments=N)

def moe_ffn(h, w_rg, b_rg, w_re, b_re, w_eg, w_eu, w_ed):
    B, T, D = h.shape
    x2 = h.reshape(-1, D)
    N = x2.shape[0]
    lg_group = (x2 @ w_rg).astype(jnp.float32) + b_rg
    p_group = jax.nn.softmax(lg_group, axis=-1)
    _, g_sel = lax.top_k(lg_group, 1)
    p_sel = jnp.take_along_axis(p_group, g_sel, axis=-1)
    lg_exp = ((x2 @ w_re).astype(jnp.float32) + b_re).reshape(N, N_GROUPS, EXPERTS_PER_GROUP)
    lg_in = lg_exp[jnp.arange(N), g_sel[:, 0]]
    top_v, top_i = lax.top_k(lg_in, TOP_K)
    gates = jax.nn.softmax(top_v, axis=-1) * p_sel
    e_idx = (g_sel * EXPERTS_PER_GROUP + top_i).astype(jnp.int32)
    y = expert_dispatch(x2, e_idx, gates, w_eg, w_eu, w_ed)
    return y.reshape(B, T, D)

def encoder_layer(x, c, past_k, past_v, past_s, g_mix, g_ffn, w_ada, b_ada, w_in, sinks,
                  w_gate_up, b_gate, g_head, w_out, w_rg, b_rg, w_re, b_re, w_eg, w_eu, w_ed):
    sh1, sc1, gt1, sh2, sc2, gt2 = adaln(c, w_ada, b_ada)
    h = modulate(rmsnorm(x, g_mix), sh1, sc1)
    qa, ka, va, qb, kb, vb, rb, lg = project_inputs(h, w_in, w_gate_up, b_gate)
    if past_k is None:
        oa = swa_prompt(qa, ka, va, sinks)
        s_new, ob = gla_prompt(qb, kb, vb, lg)
        k_state, v_state = ka[:, -WINDOW:], va[:, -WINDOW:]
    else:
        oa = swa_sample(qa, ka, va, past_k, past_v, sinks)
        s_new, ob = gla_block(past_s.astype(jnp.float32), qb, kb, vb, lg)
        k_state, v_state = ka, va
    x = x + gt1 * mixer_output(oa, ob, rb, g_head, w_out)
    h = modulate(rmsnorm(x, g_ffn), sh2, sc2)
    x = x + gt2 * moe_ffn(h, w_rg, b_rg, w_re, b_re, w_eg, w_eu, w_ed)
    return x, k_state, v_state, s_new

def setup_inputs(seed: int = 0) -> dict:
    key = jax.random.key(seed)
    ks = jax.random.split(key, 26)
    D = D_MODEL

    def nrm(k, shape, scale):
        return scale * jax.random.normal(k, shape, jnp.float32)

    return {
        'x_prompt': nrm(ks[0], (BATCH, SEQ, D), 1.0),
        'x_sample': nrm(ks[1], (DEC_BATCH, DEC_SEQ, D), 1.0),
        'cache_swa_k': nrm(ks[2], (DEPTH, DEC_BATCH, min(WINDOW, PAST_LEN), SWA_KV_HEADS, SWA_HEAD_DIM), 1.0),
        'cache_swa_v': nrm(ks[3], (DEPTH, DEC_BATCH, min(WINDOW, PAST_LEN), SWA_KV_HEADS, SWA_HEAD_DIM), 1.0),
        'state_gla': nrm(ks[4], (DEPTH, DEC_BATCH, GLA_HEADS, GLA_DK, GLA_DV), 1.0),
        'c_prompt': nrm(ks[5], (BATCH, D), 1.0),
        'c_sample': nrm(ks[6], (DEC_BATCH, D), 1.0),
        'g_mix_norm': 1.0 + nrm(ks[7], (DEPTH, D), 0.02),
        'g_ffn_norm': 1.0 + nrm(ks[8], (DEPTH, D), 0.02),
        'w_ada': nrm(ks[9], (DEPTH, D, N_MOD * D), 0.3 * D ** -0.5),
        'b_ada': nrm(ks[10], (DEPTH, N_MOD * D), 0.02),
        'w_in': nrm(ks[11], (DEPTH, D, D_IN), D ** -0.5),
        'attn_sinks': nrm(ks[12], (DEPTH, SWA_HEADS), 0.5),
        'w_gla_gate': nrm(ks[13], (DEPTH, GLA_GATE_RANK, GLA_HEADS * GLA_DK), GLA_GATE_RANK ** -0.5),
        'b_gla_gate': nrm(ks[14], (DEPTH, GLA_HEADS * GLA_DK), 0.1),
        'g_gla_norm': 1.0 + nrm(ks[15], (DEPTH, GLA_DV), 0.02),
        'w_out': nrm(ks[16], (DEPTH, D, D), D ** -0.5),
        'w_router_group': nrm(ks[17], (DEPTH, D, N_GROUPS), D ** -0.5),
        'b_router_group': nrm(ks[18], (DEPTH, N_GROUPS), 0.01),
        'w_router_expert': nrm(ks[19], (DEPTH, D, N_EXPERTS), D ** -0.5),
        'b_router_expert': nrm(ks[20], (DEPTH, N_EXPERTS), 0.01),
        'w_expert_gate': nrm(ks[21], (DEPTH, N_EXPERTS, D, EXPERT_HIDDEN), D ** -0.5),
        'w_expert_up': nrm(ks[22], (DEPTH, N_EXPERTS, D, EXPERT_HIDDEN), D ** -0.5),
        'w_expert_down': nrm(ks[23], (DEPTH, N_EXPERTS, EXPERT_HIDDEN, D), EXPERT_HIDDEN ** -0.5),
        'g_final': 1.0 + nrm(ks[24], (D,), 0.02),
    }

def reference(x_prompt, x_sample, cache_swa_k, cache_swa_v, state_gla, c_prompt, c_sample,
              g_mix_norm, g_ffn_norm, w_ada, b_ada, w_in, attn_sinks, w_gla_gate, b_gla_gate,
              g_gla_norm, w_out, w_router_group, b_router_group, w_router_expert, b_router_expert,
              w_expert_gate, w_expert_up, w_expert_down, g_final):
    xp, xs = x_prompt, x_sample
    kp, vp, sp, ksm, vsm, ssm = [], [], [], [], [], []
    for l in range(DEPTH):
        wl = (g_mix_norm[l], g_ffn_norm[l], w_ada[l], b_ada[l], w_in[l], attn_sinks[l],
              w_gla_gate[l], b_gla_gate[l], g_gla_norm[l], w_out[l], w_router_group[l],
              b_router_group[l], w_router_expert[l], b_router_expert[l], w_expert_gate[l],
              w_expert_up[l], w_expert_down[l])
        xp, k_, v_, s_ = encoder_layer(xp, c_prompt, None, None, None, *wl)
        kp.append(k_)
        vp.append(v_)
        sp.append(s_)
        xs, k_, v_, s_ = encoder_layer(xs, c_sample, cache_swa_k[l], cache_swa_v[l], state_gla[l], *wl)
        ksm.append(k_)
        vsm.append(v_)
        ssm.append(s_)
    y_prompt = rmsnorm(xp, g_final)
    y_sample = rmsnorm(xs, g_final)
    return (y_prompt, y_sample, jnp.stack(kp), jnp.stack(vp), jnp.stack(sp),
            jnp.stack(ksm), jnp.stack(vsm), jnp.stack(ssm))


_drawn_inputs = setup_inputs


def setup_inputs(seed=0):
    import zlib

    import numpy as np

    out = dict(_drawn_inputs(seed))
    spreads = {}
    factors = {'cache_swa_k': 4.038,
     'cache_swa_v': 3.251,
     'g_ffn_norm': 8.0,
     'attn_sinks': 8.0,
     'g_gla_norm': 8.0,
     'b_router_group': 8.0,
     'b_router_expert': 8.0,
     'g_final': 2.834}
    for name, (base, spread) in spreads.items():
        noise = np.random.default_rng([zlib.crc32(name.encode()), seed]).standard_normal(out[name].shape)
        drawn = base * np.exp(spread * noise) if base else spread * noise
        out[name] = __import__('jax').numpy.asarray(drawn.astype(out[name].dtype))
    for name, factor in factors.items():
        out[name] = (out[name] * factor).astype(out[name].dtype)
    return out
```

```python
from contextlib import ExitStack

import concourse.bass as bass
from concourse import mybir
from concourse.alu_op_type import AluOpType as ALU

ACT = mybir.ActivationFunctionType
AX = mybir.AxisListType
F32 = mybir.dt.float32
I32 = mybir.dt.int32
U32 = mybir.dt.uint32

P = 128
D = 2048
KC = D // P
NT = 3
TOK = NT * P
NMOD = 6
DEC_B, DEC_T = 8, 16
WIN, CHUNK, HD = 128, 64, 64
SWA_H, SWA_KV = 16, 2
DK, DV, GH, GB = 128, 256, 4, 16
NE, GRP, EPG = 32, 4, 8
HID = 512
W = 64
NOVER = 2 * TOK // W
QN = 512
EPS = 1e-6
BIG = 4096.0
NEG = -1e30
COL_KV, COL_QB, COL_VB, COL_AB = 1024, 1280, 2304, 4352

PRE = 8
RING = 12
U_ADA0 = 0
U_KVA = 2 * KC
U_T = U_KVA + 3
U_V = U_T + 48
U_ADA4 = U_V + 16
U_OUT = U_ADA4 + 32
U_MOE = U_OUT + 16
UE = 12


def wait_count(eng, sem, n):
    if not isinstance(n, int) or n > 0:
        eng.wait_ge(sem, n)


def peeled(eng, body, times, chain=None, per=0):
    body(0)
    if chain:
        chain.loop_from_one(per)
    with eng.Fori(1, times) as i:
        if chain:
            chain.enter(i, per)
        body(i)
        if chain:
            chain.leave(times)


class Chain:

    def __init__(self, eng, sem):
        self.eng, self.sem, self.n, self.extra, self.at = eng, sem, 0, 0, 0

    def __call__(self, ins):
        ins.then_inc(self.sem, 1)
        self.n += 1
        self.eng.wait_ge(self.sem, self.extra + self.n)

    def count(self, ins):
        ins.then_inc(self.sem, 1)
        self.n += 1

    def wait(self):
        self.eng.wait_ge(self.sem, self.extra + self.n)

    def loop_from_one(self, per):
        self.n -= per

    def enter(self, i, per):
        self.at, self.per, self.extra = self.n, per, i * per

    def leave(self, times):
        assert self.n - self.at == self.per, (self.n - self.at, self.per)
        self.n, self.extra = self.at + times * self.per, 0


def encoder_step(nc, A, O):
    with ExitStack() as ctx:
        def sb(name, shape, dt=F32):
            return ctx.enter_context(nc.sbuf_tensor(name, shape, dt))

        def sem(name):
            return ctx.enter_context(nc.semaphore(name))

        ring = sb("ring", [P, RING * D])
        xbuf = sb("xbuf", [P, NT * D])
        hbuf = sb("hbuf", [P, KC * TOK])
        zbuf = sb("zbuf", [P, 16 * TOK])
        dbuf = sb("dbuf", [P, 2 * D])
        kva = sb("kva", [P, NT, 256])
        modr = sb("modr", [P, NMOD, QN])
        low = sb("low", [P, 1024])
        abT = low[:, 0:TOK]
        wgate = low[:, 512:1024]
        gheadb = sb("gheadb", [P, DV])
        sinkb = sb("sinkb", [P, SWA_H])
        sinks_s = sb("sinks_s", [P, SWA_KV])
        ident = sb("ident", [P, P])
        tri_lt = sb("tri_lt", [P, P])
        ones = sb("ones", [P, P])
        sel = sb("sel", [P, 2, P])
        par_tmp = sb("par_tmp", [P, 2, 4])
        par_col = sb("par_col", [P, 2])
        iota_e = sb("iota_e", [P, NE])
        token = sb("token", [P, 2, NT])
        half = sb("half", [P, 1])
        stat = sb("stat", [P, 64])
        rs = sb("rs", [P, 3, 4])
        rt = low[:, 0:NT * 256].rearrange("p (t c) -> p t c", t=NT)
        gtab = sb("gtab", [P, NE + 1])
        stab = sb("stab", [P, NE])
        dest_i = sb("dest_i", [P, 2 * NT], I32)
        tok_i = sb("tok_i", [P, 2 * NT], I32)
        gate = sb("gate", [P, 2, NT])
        ov_f = hbuf[0:1, 4096:5120]
        ov_i = sb("ov_i", [1, 64], I32)
        cur = sb("cur", [P, 8, 1], I32)
        gcur, scur, ocur_i = cur[:, 0:2, :], cur[:, 2:4, :], cur[:, 4, :]
        ocur = stat[:, 56:60].unsqueeze(2)

        bank = [ctx.enter_context(nc.psum_tensor(f"bank{i}", [P, QN], F32)) for i in range(8)]

        h2_dram = nc.dram_tensor("h2_rows", (2 * TOK, D // 2), F32, kind="Internal").ap()
        y_dram = nc.dram_tensor("y_rows", (4 * TOK, D // 2), F32, kind="Internal").ap()
        slots_dram = nc.dram_tensor("slot_table", (NE * TOK + P, 1), I32, kind="Internal").ap()

        def unit(s):
            return ring[:, s * D:(s + 1) * D]

        arena = ring[:, PRE * D:RING * D]
        x = xbuf[:, :].rearrange("p (t d) -> p t d", t=NT)
        vr = xbuf[:, :].rearrange("p (a t c) -> p a t c", a=2, t=NT)
        hT = hbuf[:, :].rearrange("p (k n) -> p k n", k=KC)
        zT = zbuf[:, :].rearrange("p (k n) -> p k n", k=16)
        crow = zbuf[0:9, 0:D]
        ctmp = dbuf[:, 2560:2704].rearrange("p (k r) -> p k r", k=KC)
        bias = arena[:, 0:2048].rearrange("p (m c) -> p m c", m=4)
        mix_gain = arena[:, 3072:3584]
        ffn_gain = arena[:, 5120:5632]
        modT = arena[:, 7300:7588].rearrange("p (m k r) -> p m k r", m=2, k=KC)
        cT = dbuf[:, 2048:2560].rearrange("p (k r) -> p k r", k=KC)
        empty = arena[:, 7200:7297].bitcast(I32)
        tri_le = arena[:, 6144:6272]
        tri_les = arena[:, 6272:6400]
        tri_gts = arena[:, 6400:6528]
        band = arena[:, 6528:6784]
        par_row = arena[:, 6784:7040].rearrange("p (u n) -> p u n", u=2)
        dec = arena[:, 7040:7136].rearrange("p (h b) -> p h b", h=GH)
        past_kT = arena[:, 0:2048].rearrange("p (b j n) -> p b j n", b=DEC_B, j=SWA_KV)
        kT2 = arena[:, 2048:2816].rearrange("p (j n) -> p j n", j=SWA_KV)
        q_s = hbuf[:, 4096:5120].rearrange("p (b j n) -> p b j n", b=DEC_B, j=SWA_KV)
        v_new = arena[0:16, 3072:4096].rearrange("p (b c) -> p b c", b=DEC_B)
        kdup = arena[:, 5120:5888].rearrange("p (t j u c) -> p t j u c", t=NT, j=SWA_KV, u=2)
        cache_v = arena[:, 4096:5120].rearrange("p (b c) -> p b c", b=DEC_B)
        cache_k2 = dbuf[:, 0:2048].rearrange("p (b j u c) -> p b j u c", b=DEC_B, j=SWA_KV, u=2)
        sS = [dbuf[:, 0:512], dbuf[:, 2560:3072], arena[:, 7680:8192]]
        PT = dbuf[:, 3072:4096].rearrange("p (u n) -> p u n", u=2)
        lg = arena[:, 0:512]
        ebT = arena[:, 512:1024]
        enbT = arena[:, 1024:1536]
        esuf = arena[:, 1536:2048]
        kk = arena[:, 2048:3072].rearrange("p (u n) -> p u n", u=2)
        qdm = arena[:, 3072:4096].rearrange("p (u h n) -> p u h n", u=2, h=GH)
        AT = arena[:, 4096:4608]
        Sp = [zbuf[:, 1024 * u:1024 * u + 1024] for u in range(2)]
        og = dbuf[:, 0:1024]
        ogsq = arena[:, 7680:8192]
        Sin = [dbuf[:, 1024:2048], dbuf[:, 2048:3072]]
        Sout = [dbuf[:, 3072:4096], Sp[0]]
        silu_r = zbuf[:, 2048:3072]
        kflat = kva[:, :, :].rearrange("p t c -> p (t c)")
        wr = kflat[:, 0:576].rearrange("p (k c) -> p k c", k=KC)
        br = kflat[:, 576:612]
        tab_a = hbuf[:, 5120:5152].bitcast(I32)
        tab_f = hbuf[:, 5152:5248].rearrange("p (q e) -> p q e", q=3)
        gbc = dbuf[:, :].rearrange("p (q c) -> p q c", q=2)
        mul_tmp = zbuf[:, 0:1536].rearrange("p (u c) -> p u c", u=NT)
        h2 = [zbuf[:, 2048:4096], zbuf[:, 4096:6144]]
        sq_tmp = zbuf[:, 2048:6144]
        x1_parts = stat[:, 8:20].rearrange("p (t b) -> p t b", t=NT)
        xg = [zbuf[:, 1024 * u:1024 * u + 1024] for u in range(2)]
        xeT = [zbuf[:, 2048 + 1024 * u:3072 + 1024 * u].rearrange("p (c q s) -> p c q s", c=8, q=2)
               for u in range(2)]
        ysb = [zbuf[:, 4096 + 1024 * u:5120 + 1024 * u] for u in range(2)]
        sg = [hbuf[:, 256 * u:256 * u + 256] for u in range(2)]
        hid = [hbuf[:, 512 + 256 * u:768 + 256 * u] for u in range(2)]
        hidT = [hbuf[:, 1024 + 256 * u:1280 + 256 * u].rearrange("p (c q s) -> p c q s", c=2, q=2)
                for u in range(2)]
        gfin = hbuf[:, 2048:4096]
        yk = [ring[:, 4096 * t:4096 * t + 4096].rearrange("p (k d) -> p k d", k=2) for t in range(NT)]
        sqf = ring[:, 12288:14336]

        loaded = [sem(f"loaded{s}") for s in range(RING)]
        unit_used = sem("unit_used")
        x_in, c_in, small_in, cache_in, bias_in = (sem(n) for n in ("x_in", "c_in", "small_in", "cache_in", "bias_in"))
        ident_ready, gate_zero, consts = sem("ident_ready"), sem("gate_zero"), sem("consts")
        c_exp, cT_ps, cT_sb = sem("c_exp"), sem("cT_ps"), sem("cT_sb")
        xsq, xn, xT_ps, xT_sb = sem("xsq"), sem("xn"), sem("xT_ps"), sem("xT_sb")
        mods, modT_ps, modT_sb = sem("mods"), sem("modT_ps"), sem("modT_sb")
        h_prompt, h_sample = sem("h_prompt"), sem("h_sample")
        ev_a, ev_v = sem("ev_a"), sem("ev_v")
        kv_out, vnew_in = sem("kv_out"), sem("vnew_in")
        kdup_sb, kT_ps, kT_sb = sem("kdup_sb"), sem("kT_ps"), sem("kT_sb")
        sc_ps, sc_sb, nm_sb, p_exp, p_sb = sem("sc_ps"), sem("sc_sb"), sem("nm_sb"), sem("p_exp"), sem("p_sb")
        pT_ps, pT_sb, o_ps, o_sb = sem("pT_ps"), sem("pT_sb"), sem("o_ps"), sem("o_sb")
        lg_ps, lg_abs, lg_ln, lg_sb = sem("lg_ps"), sem("lg_abs"), sem("lg_ln"), sem("lg_sb")
        cum_ps, cum_exp, qk_sb, a_ps, a_sb = sem("cum_ps"), sem("cum_exp"), sem("qk_sb"), sem("a_ps"), sem("a_sb")
        s_in = [sem("s_in0"), sem("s_in1")]
        s_st = [sem("s_st0"), sem("s_st1")]
        kv_ps, s_new, inter, sp_out = sem("kv_ps"), sem("s_new"), sem("inter"), sem("sp_out")
        osq, r_exp, og_sb, ogT_ps, ogT_sb = sem("osq"), sem("r_exp"), sem("og_sb"), sem("ogT_ps"), sem("ogT_sb")
        gbc_ps, gbc_sb = sem("gbc_ps"), sem("gbc_sb")
        x_in2, x1, x1sq, x1sum = sem("x_in2"), sem("x1"), sem("x1sq"), sem("x1sum")
        bc_ps, h2_v = sem("bc_ps"), sem("h2_v")
        h2_out = [sem("h2_out0"), sem("h2_out1"), sem("h2_out2")]
        h2T_ps, h2T_sb, logit_ps = sem("h2T_ps"), sem("h2T_sb"), sem("logit_ps")
        g_arg, g_exp, rank_rdy, rank_ps, dest_rdy = sem("g_arg"), sem("g_exp"), sem("rank_rdy"), sem("rank_ps"), sem("dest_rdy")
        slots_init, slots_set, slots_in, tabs = sem("slots_init"), sem("slots_set"), sem("slots_in"), sem("tabs")
        ov_rdy, xg_zero, gfin_in = sem("ov_rdy"), sem("xg_zero"), sem("gfin_in")
        gat = [sem("gat0"), sem("gat1")]
        sct = [sem("sct0"), sem("sct1")]
        eT_ps, eT_v, eT_a = sem("eT_ps"), sem("eT_v"), sem("eT_a")
        gu_ps, gu_exp, hid_sb, hT_ps, hT_sb = sem("gu_ps"), sem("gu_exp"), sem("hid_sb"), sem("hT_ps"), sem("hT_sb")
        y_v, y_a, moe_done, y_gated = sem("y_v"), sem("y_a"), sem("moe_done"), sem("y_gated")
        yk_in = [sem("yk_in0"), sem("yk_in1"), sem("yk_in2")]
        fin_rs, fin_mul = sem("fin_rs"), sem("fin_mul")
        fin_sum, fin_sq, fin_rdy, fin_out = sem("fin_sum"), sem("fin_sq"), sem("fin_rdy"), sem("fin_out")
        rlog, rstd = sem("rlog"), sem("rstd")
        ocur_rdy = sem("ocur_rdy")
        ocur_in, router_in = sem("ocur_in"), sem("router_in")
        ch_v, ch_a, ch_p, ch_r = sem("ch_v"), sem("ch_a"), sem("ch_p"), sem("ch_r")

        w_ada, w_in, w_out = A["w_ada"][0], A["w_in"][0], A["w_out"][0]
        ada_v = w_ada.rearrange("(k p) (m c) -> p k m c", p=P, m=NMOD)
        in_v = w_in.rearrange("(k p) c -> p k c", p=P)
        out_v = w_out.rearrange("(k p) c -> p k c", p=P)
        eg_v = A["w_expert_gate"][0].rearrange("e (k p) f -> p e k f", p=P)
        eu_v = A["w_expert_up"][0].rearrange("e (k p) f -> p e k f", p=P)
        ed_v = A["w_expert_down"][0].rearrange("e (k p) d -> p e k d", p=P)
        st_v = A["state_gla"][0].rearrange("b h k v -> b k h v")
        so_v = O["gla_state_sample"][0].rearrange("b h k v -> b k h v")
        yout = [O["y_prompt"][0, 0:P, :], O["y_prompt"][0, P:2 * P, :],
                O["y_sample"].rearrange("b t d -> (b t) d")]
        y_rows = y_dram.rearrange("(k t p g) c -> t p k (g c)", k=2, t=NT, g=2)
        h2_rows = h2_dram.rearrange("(t p g) c -> t p (g c)", t=NT, g=2)

        H2_STEPS = [(q, t, q) for q in range(4) for t in range(2)] + [(4 + q, 2, q) for q in range(4)]

        LOGIT_BANK = (2, 5, 2)
        GATE_BANKS = ((3, 4, 6, 7), (0, 1, 6, 7))

        def steps_done(n):
            return 2 * n if n <= 4 else 4 + n

        def kv_bank(i, h):
            return (2, 0)[i % 2] + h // 2

        def loads_before(s):
            return len(range(s, U_MOE, PRE)) if s < PRE else 0

        block = ctx.enter_context(nc.Block())

        @block.sync
        def _(sp):
            sp.dma_start(crow[0:1, :], A["c_prompt"]).then_inc(c_in, 16)
            sp.dma_start(crow[1:9, :], A["c_sample"]).then_inc(c_in, 16)
            for t in range(2):
                sp.dma_start(x[:, t, :], A["x_prompt"][0, t * P:(t + 1) * P, :]).then_inc(x_in, 16)
            sp.dma_start(x[:, 2, :], A["x_sample"].rearrange("b t d -> (b t) d")).then_inc(x_in, 16)

            def fetch(n, src, dst=None, shift=0):
                if n >= PRE:
                    sp.wait_ge(unit_used, n - PRE + 1 + shift)
                dst = unit(n % PRE) if dst is None else dst
                sp.dma_start(dst, src).then_inc(loaded[n % PRE], 16)

            def quad(s):
                return unit(s).rearrange("p (k c) -> p k c", k=4)

            for m in range(2):
                for k in range(KC):
                    fetch(U_ADA0 + m * KC + k, ada_v[:, k, m, :])
            for q in range(2):
                n = U_KVA + q
                fetch(n, in_v[:, 8 * q:8 * q + 8, COL_KV:COL_KV + 256],
                      unit(n % PRE).rearrange("p (k c) -> p k c", k=8))
            n = U_KVA + 2
            fetch(n, in_v[:, :, COL_AB:COL_AB + 16], unit(n % PRE)[:, 0:256].rearrange("p (k c) -> p k c", k=KC))
            with sp.Fori(0, 2) as a:
                n = U_T
                for b in range(2):
                    for q in range(4):
                        fetch(n, in_v[:, 4 * q:4 * q + 4, bass.ds(a * COL_QB + QN * b, QN)], quad(n % PRE), 24 * a)
                        n += 1
                    for k in range(8 * b, 8 * b + 8):
                        fetch(n, ada_v[:, k, bass.ds(a + 2, 1), :].rearrange("p m c -> p (m c)"), None, 24 * a)
                        n += 1
            with sp.Fori(0, 2) as a:
                for b in range(2):
                    for q in range(4):
                        n = U_V + 4 * b + q
                        fetch(n, in_v[:, 4 * q:4 * q + 4, bass.ds(a * (2 * QN) + (COL_VB + QN * b), QN)],
                              quad(n % PRE), 8 * a)
            for m in range(2):
                for k in range(KC):
                    fetch(U_ADA4 + m * KC + k, ada_v[:, k, 4 + m, :])
            with sp.Fori(0, 2) as a:
                for b in range(2):
                    for q in range(4):
                        n = U_OUT + 4 * b + q
                        fetch(n, out_v[:, 4 * q:4 * q + 4, bass.ds(a * (2 * QN) + QN * b, QN)],
                              quad(n % PRE), 8 * a)

            def expert(e, first):
                for j in range(UE):
                    if first:
                        if j < PRE:
                            last = max(n for n in range(U_MOE) if n % PRE == j)
                            sp.wait_ge(unit_used, last + 1)
                        elif j == PRE:
                            sp.wait_ge(og_sb, NT)
                            sp.wait_ge(inter, 24)
                            sp.wait_ge(s_new, 24)
                            sp.wait_ge(mods, NMOD + 2)
                    else:
                        sp.wait_ge(unit_used, U_MOE + UE * (e - 1) + j + 1)
                    if j < 8:
                        src = (eg_v if j < 4 else eu_v)[:, bass.ds(e, 1), 4 * (j % 4):4 * (j % 4) + 4, :]
                        src = src.rearrange("p e k f -> p (e k) f")
                        dst = quad(j)
                    else:
                        src = ed_v[:, bass.ds(e, 1), j - 8, :].rearrange("p e d -> p (e d)")
                        dst = unit(j)
                    sp.dma_start(dst, src).then_inc(loaded[j], 16)

            expert(0, True)
            with sp.Fori(1, NE) as e:
                expert(e, False)
            sp.wait_ge(ov_rdy, 1)
            n_over = sp.value_load(ov_i[0:1, 0:1], min_val=0, max_val=NOVER)
            with sp.If(n_over > 0):
                with sp.Fori(0, n_over) as i:
                    e = sp.value_load(ov_i[0:1, bass.ds(i + 1, 1)], min_val=0, max_val=NE - 1)
                    for j in range(UE):
                        sp.wait_ge(unit_used, U_MOE + UE * (NE - 1) + UE * i + j + 1)
                        if j < 8:
                            src = (eg_v if j < 4 else eu_v)[:, bass.ds(e, 1), 4 * (j % 4):4 * (j % 4) + 4, :]
                            src = src.rearrange("p e k f -> p (e k) f")
                            dst = quad(j)
                        else:
                            src = ed_v[:, bass.ds(e, 1), j - 8, :].rearrange("p e d -> p (e d)")
                            dst = unit(j)
                        sp.dma_start(dst, src).then_inc(loaded[j], 16)
            with sp.Else():
                sp.nop()

        @block.gpsimd
        def _(pool):
            link = Chain(pool, ch_p)
            g = nc.gpsimd
            link(g.memset(ident[:, :], 0.0))
            link(g.affine_select(out=ident[:, :], in_=ident[:, :], compare_op=ALU.not_equal, fill=1.0, base=0,
                                 pattern=[[-1, P]], channel_multiplier=1))
            link(g.memset(stat[:, :], 0.0))
            g.memset(stat[:, 45:46], EPS).then_inc(ident_ready, 1)
            link(g.memset(ones[:, :], 1.0))

            def blocks(m, strict, value):
                v = m[:, :].rearrange("p (b c) -> p b c", c=GB)
                link(g.memset(m[:, :], value))
                if strict:
                    link(g.affine_select(out=v, in_=v, compare_op=ALU.is_gt, fill=0.0, base=0,
                                         pattern=[[-GB, 8], [-1, GB]], channel_multiplier=1))
                    link(g.affine_select(out=v, in_=v, compare_op=ALU.is_ge, fill=0.0, base=GB - 1,
                                         pattern=[[GB, 8], [0, GB]], channel_multiplier=-1))
                else:
                    link(g.affine_select(out=v, in_=v, compare_op=ALU.is_ge, fill=0.0, base=0,
                                         pattern=[[GB, 8], [1, GB]], channel_multiplier=-1))
                    link(g.affine_select(out=v, in_=v, compare_op=ALU.is_ge, fill=0.0, base=0,
                                         pattern=[[-GB, 8], [0, GB]], channel_multiplier=1))

            blocks(tri_le, False, 1.0)
            blocks(tri_les, False, 1.0 / 16.0)
            blocks(tri_gts, True, 1.0 / 16.0)
            link(g.memset(tri_lt[:, :], 1.0))
            link(g.affine_select(out=tri_lt[:, :], in_=tri_lt[:, :], compare_op=ALU.is_gt, fill=0.0, base=0,
                                 pattern=[[1, P]], channel_multiplier=-1))
            link(g.memset(band[:, :], 0.0))
            link(g.memset(band[0:64, 192:256], NEG))
            link(g.memset(band[64:128, 0:64], NEG))
            link(g.memset(sel[:, :, :], 0.0))
            for q in range(4):
                s0 = sel[32 * q:32 * q + 32, 0, :]
                s1 = sel[32 * q:32 * q + 32, 1, :].rearrange("p (b c) -> p b c", b=8)
                link(g.affine_select(out=s0, in_=s0, compare_op=ALU.not_equal, fill=1.0, base=0,
                                     pattern=[[0, P]], channel_multiplier=1))
                link(g.affine_select(out=s1, in_=s1, compare_op=ALU.not_equal, fill=1.0, base=-1,
                                     pattern=[[-1, 8], [0, 16]], channel_multiplier=1))
            link(g.memset(par_row[:, :, :], 0.0))
            pr = par_row[:, :, :].rearrange("p u (q v c) -> p u q v c", q=4, v=2)
            g.memset(pr[:, 0, :, 0, :], 1.0)
            link(g.memset(pr[:, 1, :, 1, :], 1.0))
            link(g.memset(par_tmp[:, :, :], 1.0))
            link(g.affine_select(out=par_tmp[:, :, :], in_=par_tmp[:, :, :], compare_op=ALU.is_ge, fill=0.0, base=0,
                                 pattern=[[-16, 2], [-32, 4]], channel_multiplier=1))
            link(g.affine_select(out=par_tmp[:, :, :], in_=par_tmp[:, :, :], compare_op=ALU.is_ge, fill=0.0, base=15,
                                 pattern=[[16, 2], [32, 4]], channel_multiplier=-1))
            link(g.tensor_add(par_tmp[:, :, 0:2], par_tmp[:, :, 0:2], par_tmp[:, :, 2:4]))
            link(g.tensor_add(par_col[:, :], par_tmp[:, :, 0], par_tmp[:, :, 1]))
            g.iota(iota_e[:, :], [[1, NE]], base=0, channel_multiplier=0, allow_small_or_imprecise_dtypes=True)
            g.iota(token[:, :, :], [[TOK, 2], [P, NT]], base=0, channel_multiplier=1, allow_small_or_imprecise_dtypes=True)
            link(g.iota(tok_i[:, :], [[TOK, 2], [P, NT]], base=0, channel_multiplier=1))
            link(g.memset(half[0:64, :], 0.0))
            link(g.memset(half[64:128, :], 1.0))
            link(g.memset(empty[:, :], int(BIG)))
            g.memset(par_tmp[:, 0, 0:1], 0.0).then_inc(consts, 1)
            bv = A["b_ada"][0].rearrange("(m g c) -> g m c", m=NMOD, g=4)
            gm = A["g_mix_norm"].rearrange("a (g c) -> g a c", g=4)
            gf = A["g_ffn_norm"].rearrange("a (g c) -> g a c", g=4)
            for q in range(4):
                r = slice(32 * q, 32 * q + 32)
                g.dma_start(bias[r, :, :], bv[q:q + 1, 0:4].broadcast_to([32, 4, QN])).then_inc(bias_in, 16)
                g.dma_start(modr[r, 4:6, :], bv[q:q + 1, 4:6].broadcast_to([32, 2, QN])).then_inc(bias_in, 16)
                g.dma_start(mix_gain[r].unsqueeze(1), gm[q:q + 1].broadcast_to([32, 1, QN])).then_inc(bias_in, 16)
            pool.wait_ge(gate_zero, 1)
            for q in range(4):
                g.dma_start(wgate[32 * q:32 * q + 16, :], A["w_gla_gate"][0]).then_inc(small_in, 16)
            g.dma_start(wgate[16:17, :], A["b_gla_gate"]).then_inc(small_in, 16)
            g.dma_start(gheadb[:, :], A["g_gla_norm"].broadcast_to([P, DV])).then_inc(small_in, 16)
            g.dma_start(sinkb[:, :], A["attn_sinks"].broadcast_to([P, SWA_H])).then_inc(small_in, 16)
            sk = A["attn_sinks"].rearrange("a (j h u) -> u h a j", j=SWA_KV, u=2)
            for u in range(2):
                for h in range(4):
                    r = 64 * u + 16 * h
                    g.dma_start(sinks_s[r:r + 16, :], sk[u, h].broadcast_to([16, SWA_KV]),
                                allow_slow_non_contiguous=True).then_inc(small_in, 16)
            ck = A["cache_swa_k"][0].rearrange("b w j c -> w b j c")
            for u in range(2):
                for j in range(SWA_KV):
                    g.dma_start(cache_k2[:, :, j, u, :], ck[:, :, j, :]).then_inc(cache_in, 16)
            g.dma_start(cache_v[:, :, :], A["cache_swa_v"][0].rearrange("b w j c -> w b (j c)")).then_inc(cache_in, 16)

            g.dma_start(slots_dram.rearrange("(p c) a -> p (c a)", p=P), empty[:, :]).then_inc(slots_init, 16)

            pool.wait_ge(ev_a, 1)
            pool.wait_ge(ev_v, 1)
            for name, c in (("swa_k", 0), ("swa_v", 128)):
                g.dma_start(O[name + "_prompt"][0, 0].rearrange("w j c -> w (j c)"), kva[:, 1, c:c + 128]).then_inc(kv_out, 16)
                g.dma_start(O[name + "_sample"][0].rearrange("b t j c -> (b t) (j c)"), kva[:, 2, c:c + 128]).then_inc(kv_out, 16)
            pool.wait_ge(kv_out, 64)
            pool.wait_ge(mods, 3)
            g.dma_start(v_new[:, :, :], O["swa_v_sample"][0].rearrange("b t j c -> t b (j c)")).then_inc(vnew_in, 16)
            pool.wait_ge(o_sb, 24)
            g.dma_start(wr[:, :, 0:GRP], A["w_router_group"][0].rearrange("(k p) c -> p k c", p=P)).then_inc(router_in, 16)
            g.dma_start(wr[:, :, GRP:], A["w_router_expert"][0].rearrange("(k p) c -> p k c", p=P)).then_inc(router_in, 16)
            g.dma_start(br[:, 0:GRP], A["b_router_group"].broadcast_to([P, GRP])).then_inc(router_in, 16)
            g.dma_start(br[:, GRP:], A["b_router_expert"].broadcast_to([P, NE])).then_inc(router_in, 16)
            for q in range(4):
                g.dma_start(ffn_gain[32 * q:32 * q + 32].unsqueeze(1), gf[q:q + 1].broadcast_to([32, 1, QN])).then_inc(router_in, 16)
            pool.wait_ge(mods, 7)
            for b in range(DEC_B):
                u = b % 2
                if b >= 2:
                    pool.wait_ge(inter, 16 + b - 1)
                    pool.wait_ge(s_new, 16 + b - 1)
                g.dma_start(Sin[u].rearrange("p (h v) -> p h v", h=GH), st_v[b]).then_inc(s_in[u], 16)
                if b == 1:
                    pool.wait_ge(s_new, 16)
                    g.dma_start(O["gla_state_prompt"][0, 0].rearrange("h k v -> k h v"),
                                Sp[0].rearrange("p (h v) -> p h v", h=GH)).then_inc(sp_out, 16)
                if b >= 1:
                    pool.wait_ge(s_new, 16 + b)
                    g.dma_start(so_v[b - 1], Sout[(b - 1) % 2].rearrange("p (h v) -> p h v", h=GH)).then_inc(s_st[(b - 1) % 2], 16)
            pool.wait_ge(s_new, 24)
            g.dma_start(so_v[7], Sout[1].rearrange("p (h v) -> p h v", h=GH)).then_inc(s_st[1], 16)
            pool.wait_ge(s_st[0], 64)
            pool.wait_ge(s_st[1], 64)
            pool.wait_ge(og_sb, NT)
            for t in range(2):
                g.dma_start(x[:, t, :], A["x_prompt"][0, t * P:(t + 1) * P, :]).then_inc(x_in2, 16)
            g.dma_start(x[:, 2, :], A["x_sample"].rearrange("b t d -> (b t) d")).then_inc(x_in2, 16)
            for t in range(NT):
                pool.wait_ge(h2_v, 8 if t < 2 else 12)
                g.dma_start(h2_rows[t], h2[t % 2]).then_inc(h2_out[t], 16)
            pool.wait_ge(slots_init, 16)
            pool.wait_ge(dest_rdy, 1)
            for c in range(2 * NT):
                g.indirect_dma_start(slots_dram, bass.IndirectOffsetOnAxis(dest_i[:, c:c + 1].bitcast(U32), 0),
                                     tok_i[:, c:c + 1], None).then_inc(slots_set, 16)
            pool.wait_ge(slots_set, 16 * 2 * NT)
            tv = slots_dram[0:NE * TOK].rearrange("(e s) a -> s (e a)", e=NE)
            for q in range(2):
                g.dma_start(tab_a[64 * q:64 * q + 64, :], tv[0:W, :], allow_slow_non_contiguous=True).then_inc(slots_in, 16)
            for t in range(NT):
                pool.wait_ge(h2_out[t], 16)
            pool.wait_ge(logit_ps, NT)
            g.dma_start(gfin, A["g_final"].unsqueeze(0).broadcast_to([P, D])).then_inc(gfin_in, 16)
            for u in range(2):
                link(g.memset(xg[u], 0.0))
            pool.wait_ge(tabs, 1)

            rows_max, pairs_max = pool.to_reg(2 * TOK - 1), pool.to_reg(4 * TOK - 1)

            def settle(c):
                link.count(g.tensor_tensor(stat[0:1, 60 + c:61 + c], stat[0:1, 62:63], stat[0:1, 62:63], ALU.add))

            def gather(idx, u):
                settle(0)
                g.indirect_dma_start(xg[u], None, h2_dram, bass.IndirectOffsetOnAxis(idx.bitcast(U32), 0),
                                     bounds_check=rows_max, oob_is_err=False).then_inc(gat[u], 16)

            def scatter(idx, u):
                settle(1)
                g.indirect_dma_start(y_dram, bass.IndirectOffsetOnAxis(idx.bitcast(U32), 0), ysb[u], None,
                                     bounds_check=pairs_max, oob_is_err=False).then_inc(sct[u], 16)

            link(g.memset(cur[:, :, :], 0))

            def column(out, tab, c):
                link(g.tensor_copy(out, tab[:, bass.ds(c, 1)]))

            column(gcur[:, 0, :], gtab, 0)
            gather(gcur[:, 0, :], 0)

            def expert_rows(i):
                for u in range(2):
                    wait_count(pool, eT_ps, 2 * i + u)
                    column(gcur[:, 1 - u, :], gtab, 2 * i + (u + 1))
                    gather(gcur[:, 1 - u, :], 1 - u)
                    pool.wait_ge(y_v, 2 * i + (u + 1))
                    pool.wait_ge(y_a, 2 * i + (u + 1))
                    column(scur[:, u, :], stab, 2 * i + u)
                    scatter(scur[:, u, :], u)

            peeled(pool, expert_rows, NE // 2, link, 8)
            link.wait()
            pool.wait_ge(gat[0], 16 * 17)
            pool.wait_ge(ov_rdy, 1)
            pool.wait_ge(sct[0], 16 * 16)
            pool.wait_ge(sct[1], 16 * 16)
            n_over = pool.value_load(ov_i[0:1, 0:1], min_val=0, max_val=NOVER)
            with pool.If(n_over > 0):
                with pool.Fori(0, n_over) as i:
                    link.enter(i, 2)
                    at = pool.value_load(ov_i[0:1, bass.ds(i + 1 + NOVER, 1)], min_val=0, max_val=NE * TOK)
                    for q in range(2):
                        g.dma_start(cur[64 * q:64 * q + 64, 4, :], slots_dram[bass.ds(at, W), :]).then_inc(ocur_in, 16)
                    pool.wait_ge(ocur_rdy, i + 1)
                    gather(gcur[:, 0, :], 0)
                    pool.wait_ge(y_v, NE + 1 + i)
                    pool.wait_ge(y_a, NE + 1 + i)
                    scatter(scur[:, 0, :], 0)
                    link.wait()
                    pool.wait_ge(sct[0], 16 * 17 + 16 * i)
                    pool.wait_ge(gat[0], 16 * 18 + 16 * i)
            with pool.Else():
                pool.nop()
            pool.nop().then_inc(moe_done, 1)
            for t in range(NT):
                pool.wait_ge(fin_rdy, t + 1)
                if t < 2:
                    g.tensor_tensor(x[:, t, :], x[:, t, :], gfin, ALU.mult).then_inc(fin_mul, 1)
                    pool.wait_ge(fin_mul, t + 1)
                g.dma_start(yout[t], x[:, t, :]).then_inc(fin_out, 16)
            pool.wait_ge(fin_out, 16 * NT)
            pool.wait_ge(sp_out, 16)
            pool.wait_ge(kv_out, 64)

        @block.tensor
        def _(pe):
            mm, tr = nc.tensor.matmul, nc.tensor.transpose
            pe.wait_ge(ident_ready, 1)
            pe.wait_ge(c_in, 32)
            for k in range(KC):
                last = tr(bank[5][:, 9 * k:9 * k + 9], crow[:, k * P:(k + 1) * P], ident[0:9, 0:9])
            last.then_inc(cT_ps, 1)
            pe.wait_ge(cT_sb, 1)

            def x_T(n):
                t, q = n // 4, n % 4
                pe.wait_ge(xn, t + 1)
                if n >= 2:
                    pe.wait_ge(xT_sb, n - 1)
                for k in range(4):
                    last = tr(bank[6 + n % 2][:, k * P:(k + 1) * P], x[:, t, (4 * q + k) * P:(4 * q + k + 1) * P], ident[:, :])
                last.then_inc(xT_ps, 1)

            def landed(n, extra=0):
                pe.wait_ge(loaded[n % PRE], 16 * (n // PRE + 1) + extra)

            def ada(b, n, k, extra=0):
                landed(n, extra)
                for q in range(4):
                    last = mm(bank[b][32 * q:32 * q + 32, :], cT[:, k, :], unit(n % PRE)[:, q * QN:(q + 1) * QN],
                              start=(k == 0), stop=(k == KC - 1))
                last.then_inc(unit_used, 1)

            for m in range(2):
                for k in range(KC):
                    n = m * KC + k
                    ada(4 + m, n, k)
                    if n >= 8 and n % 2 == 0:
                        x_T((n - 8) // 2)
            for m in range(2):
                pe.wait_ge(mods, 1 + 2 * m)
                if m == 0:
                    pe.wait_ge(xT_sb, 12)
                for c in range(4):
                    last = tr(bank[6 + m][:, c * P:(c + 1) * P], modr[:, m, c * P:(c + 1) * P], ident[:, :])
                last.then_inc(modT_ps, 1)

            def h_chunk(k):
                pe.wait_ge(h_prompt, k + 1)
                pe.wait_ge(h_sample, 2 * (k // 4) + 2)

            for q in range(2):
                n = U_KVA + q
                landed(n)
                w = unit(n % PRE).rearrange("p (k c) -> p k c", k=8)
                for kk_ in range(8):
                    k = 8 * q + kk_
                    h_chunk(k)
                    for t in range(NT):
                        last = mm(bank[t][:, 0:256], hT[:, k, t * P:(t + 1) * P], w[:, kk_, :],
                                  start=(k == 0), stop=(k == KC - 1))
                last.then_inc(unit_used, 1)
            n = U_KVA + 2
            landed(n)
            w = unit(n % PRE)[:, 0:256].rearrange("p (k c) -> p k c", k=KC)
            for k in range(KC):
                r = 32 * (k % 4)
                last = mm(bank[3][r:r + 16, 0:TOK], w[:, k, :], hT[:, k, :], start=(k < 4), stop=(k >= KC - 4))
            last.then_inc(unit_used, 1)

            def block_T(n, extra):
                for q in range(4):
                    landed(n + q, extra)
                    w = unit((n + q) % PRE).rearrange("p (k c) -> p k c", k=4)
                    for kk_ in range(4):
                        k = 4 * q + kk_
                        for c in range(4):
                            last = mm(bank[c][:, 0:TOK], w[:, kk_, c * P:(c + 1) * P], hT[:, k, :],
                                      start=(k == 0), stop=(k == KC - 1))
                    last.then_inc(unit_used, 1)

            def block_V(n, extra):
                for q in range(4):
                    landed(n + q, extra)
                    w = unit((n + q) % PRE).rearrange("p (k c) -> p k c", k=4)
                    for kk_ in range(4):
                        k = 4 * q + kk_
                        for t in range(NT):
                            last = mm(bank[t][:, :], hT[:, k, t * P:(t + 1) * P], w[:, kk_, :],
                                      start=(k == 0), stop=(k == KC - 1))
                    last.then_inc(unit_used, 1)

            with pe.Fori(0, 2) as a:
                for b in range(2):
                    pe.wait_ge(ev_a, 2 * a + (1 + b))
                    pe.wait_ge(ev_v, 2 * a + (1 + b))
                    block_T(U_T + 12 * b, 48 * a)
                    if b == 0:
                        pe.wait_ge(mods, a + 3)
                    for k in range(8 * b, 8 * b + 8):
                        ada(4, U_T + 4 + 4 * b + k, k, 48 * a)
            with pe.Fori(0, 2) as a:
                for b in range(2):
                    pe.wait_ge(ev_a, 2 * a + (5 + b))
                    pe.wait_ge(ev_v, 2 * a + (5 + b))
                    block_V(U_V + 4 * b, 16 * a)
            pe.wait_ge(kdup_sb, 1)
            pe.wait_ge(cache_in, 80)
            pe.wait_ge(mods, 5)
            pe.wait_ge(ev_a, 9)
            pe.wait_ge(ev_v, 9)
            for j in range(SWA_KV):
                for t in range(NT):
                    last = tr(bank[j][:, t * P:(t + 1) * P], kdup[:, t, j, :, :].rearrange("p u c -> p (u c)"), ident[:, :])
            for q in range(4):
                for i in range(4):
                    b, j = (4 * q + i) // 2, i % 2
                    last = tr(bank[2 + q][:, i * P:(i + 1) * P], cache_k2[:, b, j, :, :].rearrange("p u c -> p (u c)"), ident[:, :])
            last.then_inc(kT_ps, 1)
            pe.wait_ge(kT_sb, 1)

            def scores(s):
                if s >= 2:
                    pe.wait_ge(sc_sb, s - 1)
                for u in range(2):
                    out = bank[2 * (s % 2) + u]
                    r = slice(64 * u, 64 * u + 64)
                    if s < 16:
                        t, m = s // 8, s % 8
                        nk = P * (t + 1)
                        last = mm(out[:, 0:nk], zT[r, m, t * P:(t + 1) * P], kT2[r, m // 4, 0:nk], start=True, stop=True)
                    else:
                        b = s - 16
                        for j in range(SWA_KV):
                            q = q_s[r, b, j, :]
                            mm(out[r, 144 * j:144 * j + 128], q, past_kT[r, b, j, :], start=True, stop=True)
                            last = mm(out[r, 144 * j + 128:144 * j + 144], q, kT2[r, j, 256 + 16 * b:272 + 16 * b],
                                      start=True, stop=True)
                last.then_inc(sc_ps, 1)

            def probs_T(s):
                pe.wait_ge(p_sb, s + 1)
                if s >= 2:
                    pe.wait_ge(pT_sb, s - 1)
                out = bank[4 + s % 2]
                p = sS[s % 3]
                if s < 16:
                    nk = P * (s // 8 + 1)
                    for u in range(2):
                        for kt in range(nk // P):
                            last = tr(out[:, (2 * u + kt) * P:(2 * u + kt + 1) * P],
                                      p[:, u * nk + kt * P:u * nk + (kt + 1) * P], ident[:, :])
                else:
                    for j in range(SWA_KV):
                        tr(out[:, j * P:(j + 1) * P], p[:, 144 * j:144 * j + 128], ident[:, :])
                        last = tr(out[0:16, 256 + j * P:256 + (j + 1) * P], p[:, 144 * j + 128:144 * j + 144], ident[:, :])
                last.then_inc(pT_ps, 1)

            def values(s):
                pe.wait_ge(pT_sb, s + 1)
                if s:
                    pe.wait_ge(o_sb, s)
                if s == 16:
                    pe.wait_ge(vnew_in, 16)
                out = bank[6]
                for u in range(2):
                    r = slice(64 * u, 64 * u + 64)
                    if s < 16:
                        t, m = s // 8, s % 8
                        j = m // 4
                        for kt in range(t + 1):
                            last = mm(out[r, 0:P], kva[:, kt, 128 + 64 * j:192 + 64 * j],
                                      PT[:, s % 2, (2 * u + kt) * P:(2 * u + kt + 1) * P], start=(kt == 0), stop=(kt == t))
                    else:
                        b = s - 16
                        for j in range(SWA_KV):
                            mm(out[r, 64 * j:64 * j + 64], cache_v[:, b, 64 * j:64 * j + 64],
                               PT[:, s % 2, j * P + 64 * u:j * P + 64 * u + 64], start=True, stop=False)
                            last = mm(out[r, 64 * j:64 * j + 64], v_new[:, b, 64 * j:64 * j + 64],
                                      PT[0:16, s % 2, 256 + j * P + 64 * u:256 + j * P + 64 * u + 64], start=False, stop=True)
                last.then_inc(o_ps, 1)

            for s in range(24 + 3):
                if s < 24:
                    scores(s)
                if 0 <= s - 2 < 24:
                    probs_T(s - 2)
                for n in range(min(32 * s // 26, 32), min(32 * (s + 1) // 26, 32)):
                    if n == KC:
                        pe.wait_ge(mods, 6)
                    ada(7, U_ADA4 + n, n % KC)
                if 0 <= s - 3 < 24:
                    values(s - 3)
            pe.wait_ge(consts, 1)
            pe.wait_ge(small_in, 16 * 15)
            pe.wait_ge(o_sb, 24)

            def gate_logits(t):
                mm(bank[2][:, :], abT[:, t * P:(t + 1) * P], wgate, start=True, stop=True).then_inc(lg_ps, 1)

            def cumulated(t):
                pe.wait_ge(lg_sb, t + 1)
                if t:
                    pe.wait_ge(s_new, 8 * t)
                for h in range(GH):
                    mm(bank[1][:, h * P:(h + 1) * P], lg[:, h * P:(h + 1) * P], tri_les[:, :], start=True, stop=True)
                mm(bank[2][:, :], tri_gts[:, :], lg, start=True, stop=True)
                for h in range(GH):
                    last = tr(bank[3][:, h * P:(h + 1) * P], zT[:, 12 + h, t * P:(t + 1) * P], ident[:, :])
                last.then_inc(cum_ps, 1)

            gate_logits(0)
            cumulated(0)
            for t in range(NT):
                cols = slice(t * P, (t + 1) * P)
                pe.wait_ge(qk_sb, t + 1)
                for h in range(GH):
                    last = mm(bank[0][:, h * P:(h + 1) * P], zT[:, 12 + h, cols], zT[:, 8 + h, cols], start=True, stop=True)
                last.then_inc(a_ps, 1)
                pe.wait_ge(a_sb, t + 1)
                if t:
                    pe.wait_ge(ogT_sb, 2 * t)
                for h in range(GH):
                    mm(bank[4 + h][:, 0:DV], AT[:, h * P:(h + 1) * P], vr[:, 0, t, h * DV:(h + 1) * DV],
                       start=True, stop=False, skip_group_check=True)
                def outer(i):
                    q = slice(32 * (i // 2), 32 * (i // 2) + 32)
                    for h in range(GH):
                        last = mm(bank[kv_bank(i, h)][:, (h % 2) * DV:(h % 2 + 1) * DV], kk[q, i % 2, h * P:(h + 1) * P],
                                  vr[q, 0, t, h * DV:(h + 1) * DV], start=True, stop=True)
                    last.then_inc(kv_ps, 1)

                outer(0)
                for i in range(8):
                    B = 8 * t + i
                    q = slice(32 * (i // 2), 32 * (i // 2) + 32)
                    u = i % 2
                    if B:
                        pe.wait_ge(s_new, B)
                    if i < 7:
                        outer(i + 1)
                    if t < 2:
                        S = Sp[B % 2]
                    else:
                        pe.wait_ge(s_in[u], 16 * (i // 2 + 1))
                        S = Sin[u]
                    for h in range(GH):
                        last = mm(bank[4 + h][q, 0:DV], qdm[:, u, h, q], S[:, h * DV:(h + 1) * DV],
                                  start=False, stop=(u == 1), skip_group_check=True)
                    last.then_inc(inter, 1)
                if t + 1 < NT:
                    gate_logits(t + 1)
                    cumulated(t + 1)
                pe.wait_ge(og_sb, t + 1)
                for c in range(8):
                    last = tr(bank[4 + c // 4][:, (c % 4) * P:(c % 4 + 1) * P], og[:, c * P:(c + 1) * P], ident[:, :])
                    if c % 4 == 3:
                        last.then_inc(ogT_ps, 1)

            def spread(m, banks, before):
                for kind in range(2):
                    for q in range(4):
                        if kind:
                            pe.wait_ge(gbc_sb, before + q + 1)
                        r = slice(32 * q, 32 * q + 32)
                        mm(bank[banks[q]][:, :], sel[r, kind, :], modr[r, m, :], start=True, stop=True).then_inc(gbc_ps, 1)

            pe.wait_ge(ogT_sb, 2 * NT)
            spread(2, GATE_BANKS[0], 0)
            with pe.Fori(0, 2) as a:
                for b in range(2):
                    for q in range(4):
                        n = U_OUT + 4 * b + q
                        landed(n, 16 * a)
                        w = unit(n % PRE).rearrange("p (k c) -> p k c", k=4)
                        if q == 0:
                            pe.wait_ge(x1, a + 1 if b == 0 else 2 * a + 1)
                            if b:
                                pe.wait_ge(gbc_sb, 8)
                        for kk_ in range(4):
                            k = 4 * q + kk_
                            for t in range(NT):
                                last = mm(bank[3 * b + t][:, :], hT[:, k, t * P:(t + 1) * P], w[:, kk_, :],
                                          start=(k == 0), stop=(k == KC - 1))
                        last.then_inc(unit_used, 1)
            pe.wait_ge(router_in, 128)
            pe.wait_ge(mods, NMOD + 2)

            def spread_norm(n):
                if n == 0:
                    pe.wait_ge(gbc_sb, 8)
                if n == 1:
                    pe.wait_ge(x1, 5)
                if n >= 2:
                    pe.wait_ge(h2_v, steps_done(n - 1))
                r = slice(32 * (n % 4), 32 * (n % 4) + 32)
                b = 6 - 3 * (n % 2)
                mm(bank[b][:, :], sel[r, n // 4, :], modr[r, 4, :], start=True, stop=True)
                mm(bank[b + 1][:, :], sel[r, n // 4, :], modr[r, 3, :], start=True, stop=True).then_inc(bc_ps, 1)

            def logits(t):
                pe.wait_ge(h2T_sb, 8 if t < 2 else 12)
                if t == 2:
                    pe.wait_ge(rank_rdy, 1)
                for k in range(KC):
                    last = mm(bank[LOGIT_BANK[t]][:, 64 * t:64 * t + GRP + NE], hT[:, k, t * P:(t + 1) * P], wr[:, k, :],
                              start=(k == 0), stop=(k == KC - 1))
                last.then_inc(logit_ps, 1)

            spread_norm(0)
            spread_norm(1)
            for s, (n, t, q) in enumerate(H2_STEPS):
                pe.wait_ge(h2_v, s + 1)
                if s == 0:
                    pe.wait_ge(x1, 5)
                if s >= 2:
                    pe.wait_ge(h2T_sb, s - 1)
                for k in range(4):
                    last = tr(bank[s % 2][:, k * P:(k + 1) * P], h2[t % 2][:, (4 * q + k) * P:(4 * q + k + 1) * P], ident[:, :])
                last.then_inc(h2T_ps, 1)
                if t and n + 2 < 8:
                    spread_norm(n + 2)
                if s == 9:
                    logits(0)
                    logits(1)
            logits(2)
            pe.wait_ge(rank_rdy, NT)
            for t in range(NT):
                for b in range(t + 1):
                    mm(bank[5][:, t * NE:(t + 1) * NE], (tri_lt if b == t else ones)[:, :], rt[:, b, 96:128],
                       start=(b == 0), stop=(b == t))
            for b in range(NT):
                last = mm(bank[5][:, 3 * NE:4 * NE], ones[:, :], rt[:, b, 96:128], start=(b == 0), stop=(b == NT - 1))
            last.then_inc(rank_ps, 1)
            pe.wait_ge(h2_v, 12)
            spread(5, GATE_BANKS[1], 8)
            pe.wait_ge(dest_rdy, 1)
            pe.wait_ge(ov_rdy, 1)
            pe.wait_ge(gbc_sb, 16)

            def rows_T(u, e, gat_need):
                pe.wait_ge(gat[u], gat_need)
                for c in range(8):
                    last = tr(bank[c // 4][:, (c % 4) * P:(c % 4 + 1) * P], xg[u][:, c * P:(c + 1) * P], ident[:, :])
                last.then_inc(eT_ps, 1)

            def expert_landed(j, e):
                pe.wait_ge(loaded[j], 16 * loads_before(j) + 16 + e * 16)

            def up(u, e, t_need):
                pe.wait_ge(eT_v, t_need)
                pe.wait_ge(eT_a, t_need)
                for j in range(8):
                    expert_landed(j, e)
                    w = unit(j).rearrange("p (k f) -> p k f", k=4)
                    for kk_ in range(4):
                        k = 4 * (j % 4) + kk_
                        for q in range(2):
                            last = mm(bank[2 + u][64 * q:64 * q + 64, 256 * (j // 4):256 * (j // 4) + 256],
                                      xeT[u][:, k % 8, k // 8, :], w[:, kk_, 256 * q:256 * q + 256],
                                      start=(k == 0), stop=(k == KC - 1))
                    last.then_inc(unit_used, 1)

            def hidden_T(u, e):
                pe.wait_ge(hid_sb, e + 1)
                for c in range(2):
                    last = tr(bank[4][:, c * P:(c + 1) * P], hid[u][:, c * P:(c + 1) * P], ident[:, :])
                last.then_inc(hT_ps, 1)

            def down(u, e):
                pe.wait_ge(hT_sb, e + 1)
                wait_count(pe, y_v, e)
                wait_count(pe, y_a, e)
                for k in range(4):
                    expert_landed(8 + k, e)
                    for n in range(2):
                        for q in range(2):
                            last = mm(bank[5 + n][64 * q:64 * q + 64, :], hidT[u][:, k % 2, k // 2, :],
                                      unit(8 + k)[:, 1024 * q + QN * n:1024 * q + QN * n + QN],
                                      start=(k == 0), stop=(k == 3))
                    last.then_inc(unit_used, 1)

            rows_T(0, 0, 16)

            def two_experts(i):
                for u in range(2):
                    e = 2 * i + u
                    up(u, e, e + 1)
                    rows_T(1 - u, e + 1, 16 * i + 16 * (1 + u))
                    hidden_T(u, e)
                    down(u, e)

            peeled(pe, two_experts, NE // 2)
            n_over = pe.value_load(ov_i[0:1, 0:1], min_val=0, max_val=NOVER)
            with pe.If(n_over > 0):
                with pe.Fori(0, n_over) as i:
                    e = i + NE
                    rows_T(0, e + 1, 16 * 18 + 16 * i)
                    up(0, e, e + 2)
                    hidden_T(0, e)
                    down(0, e)
            with pe.Else():
                pe.nop()

        @block.scalar
        def _(act):
            link = Chain(act, ch_a)
            af = nc.scalar.activation
            cp = nc.scalar.copy

            def inv_rms(sq, n_done, cols, out, n):
                act.wait_ge(sq, n_done)
                af(rs[:, 0, out], stat[:, cols], ACT.Ln, scale=1.0 / n, bias=stat[:, 45:46]).then_inc(rlog, 1)
                rcount[0] += 1
                act.wait_ge(rlog, rcount[0])
                af(rs[:, 0, out], rs[:, 0, out], ACT.Exp, scale=-0.5).then_inc(rstd, 1)

            rcount = [0]
            act.wait_ge(cT_ps, 1)
            af(ctmp.rearrange("p k r -> p (k r)"), bank[5][:, 0:9 * KC], ACT.Exp, scale=-1.0).then_inc(c_exp, 1)
            for t in range(NT):
                act.wait_ge(x_in, 48)
                if t == 0:
                    act.wait_ge(ident_ready, 1)
                if t:
                    act.wait_ge(xsq, t)
                af(hbuf[:, 0:D], x[:, t, :], ACT.Square, accum_out=stat[:, t:t + 1]).then_inc(xsq, 1)
            inv_rms(xsq, 3, slice(0, NT), slice(0, NT), D)
            for n in range(12):
                t, q = n // 4, n % 4
                act.wait_ge(xT_ps, n + 1)
                cp(hT[:, 4 * q:4 * q + 4, t * P:(t + 1) * P], bank[6 + n % 2][:, :].rearrange("p (k c) -> p k c", k=4)).then_inc(xT_sb, 1)
            act.wait_ge(modT_sb, 2)
            act.wait_ge(xT_sb, 12)
            for k in range(KC):
                af(hT[:, k, 0:2 * P], hT[:, k, 0:2 * P], ACT.Identity, scale=modT[:, 1, k, 0:1], bias=modT[:, 0, k, 0:1]).then_inc(h_prompt, 1)
            act.wait_ge(unit_used, U_KVA + 3)
            cp(kva[:, 0, :], bank[0][:, 0:256])
            cp(kva[:, 1, :], bank[1][:, 0:256]).then_inc(ev_a, 1)
            with act.Fori(0, 2) as a:
                for b in range(2):
                    act.wait_ge(unit_used, 24 * a + (U_T + 12 * b + 4))
                    for c in range(2):
                        last = cp(zT[:, bass.ds(8 * a + (4 * b + c), 1), :].rearrange("p a n -> p (a n)"), bank[c][:, 0:TOK])
                    last.then_inc(ev_a, 1)
            vflat = xbuf[:, :].rearrange("p (a c) -> p a c", a=2)
            with act.Fori(0, 2) as a:
                for b in range(2):
                    act.wait_ge(unit_used, 8 * a + (U_V + 4 * b + 4))
                    for c in range(2):
                        last = cp(vflat[:, bass.ds(a, 1), 1024 * c + QN * b:1024 * c + QN * b + QN].rearrange("p a n -> p (a n)"), bank[c][:, :])
                    last.then_inc(ev_a, 1)
            act.wait_ge(kT_ps, 1)
            for q in range(4):
                last = cp(past_kT[:, 2 * q:2 * q + 2, :, :].rearrange("p b j n -> p (b j n)"), bank[2 + q][:, :])
            link(nc.scalar.copy(stat[:, 40:41], stat[:, 0:1]))
            for s in range(24 + 3):
                if s < 24:
                    act.wait_ge(nm_sb, s + 1)
                    st = stat[:, 8 + 8 * (s % 2):16 + 8 * (s % 2)]
                    n = (P * (s // 8 + 1)) if s < 16 else 144
                    for u in range(2):
                        p = sS[s % 3][:, u * n:(u + 1) * n]
                        af(p, p, ACT.Exp, bias=st[:, u:u + 1], accum_out=st[:, 4 + u:5 + u])
                    af(st[:, 2:4], st[:, 2:4], ACT.Exp).then_inc(p_exp, 1)
                if 0 <= s - 2 < 24:
                    r = s - 2
                    act.wait_ge(pT_ps, r + 1)
                    if r >= 2:
                        act.wait_ge(o_ps, r - 1)
                    src, dst = bank[4 + r % 2], PT[:, r % 2, :]
                    if r < 8:
                        v = lambda a: a.rearrange("p (u k n) -> p u k n", u=2, k=2)[:, :, 0, :]
                        cp(v(dst), v(src[:, :])).then_inc(pT_sb, 1)
                    elif r < 16:
                        cp(dst, src[:, :]).then_inc(pT_sb, 1)
                    else:
                        cp(dst[:, 0:256], src[:, 0:256])
                        cp(dst[0:16, 256:512], src[0:16, 256:512]).then_inc(pT_sb, 1)
                if 0 <= s - 3 < 24:
                    r = s - 3
                    act.wait_ge(o_ps, r + 1)
                    src = bank[6][:, 0:P]
                    if r < 16:
                        cp(hT[:, r % 8, (r // 8) * P:(r // 8 + 1) * P], src).then_inc(o_sb, 1)
                    else:
                        b = r - 16
                        cp(hT[:, 0:8, 256 + 16 * b:272 + 16 * b], src.rearrange("p (c n) -> p c n", c=8)).then_inc(o_sb, 1)

            def log1p_exp(t):
                act.wait_ge(lg_abs, t + 1)
                link(af(lg, lg, ACT.Exp, scale=-1.0))
                af(lg, lg, ACT.Ln, bias=1.0).then_inc(lg_ln, 1)

            def cum_exps(t):
                act.wait_ge(cum_ps, t + 1)
                af(ebT, bank[1][:, :], ACT.Exp)
                af(enbT, bank[1][:, :], ACT.Exp, scale=-1.0)
                af(esuf, bank[2][:, :], ACT.Exp).then_inc(cum_exp, 1)
                if t:
                    act.wait_ge(og_sb, t)
                af(silu_r, vr[:, 1, t, :], ACT.Exp, scale=-1.0).then_inc(r_exp, 1)

            log1p_exp(0)
            cum_exps(0)
            for t in range(NT):
                act.wait_ge(inter, 8 * t + 8)
                for h in range(GH):
                    last = af(ogsq[:, (h % 2) * DV:(h % 2 + 1) * DV], bank[4 + h][:, 0:DV], ACT.Square, accum_out=stat[:, 48 + h:49 + h])
                    if h % 2 and h < 3:
                        link(last)
                last.then_inc(osq, 1)
                if t + 1 < NT:
                    log1p_exp(t + 1)
                inv_rms(osq, t + 1, slice(48, 52), slice(0, 4), DV)
                if t + 1 < NT:
                    cum_exps(t + 1)
                for q in range(2):
                    act.wait_ge(ogT_ps, 2 * t + q + 1)
                    cp(hT[:, 8 + 4 * q:12 + 4 * q, t * P:(t + 1) * P], bank[4 + q][:, :].rearrange("p (k c) -> p k c", k=4)).then_inc(ogT_sb, 1)
            act.wait_ge(s_st[0], 64)
            act.wait_ge(s_st[1], 64)
            for n in range(8):
                act.wait_ge(gbc_ps, n + 1)
                cp(gbc[:, n // 4, (n % 4) * QN:(n % 4 + 1) * QN], bank[GATE_BANKS[0][n % 4]][:, :]).then_inc(gbc_sb, 1)
            for b in range(4):
                act.wait_ge(x1, b + 2)
                for t in range(NT):
                    n = NT * b + t
                    if n >= 8:
                        act.wait_ge(x1sq, n - 7)
                    af(sq_tmp[:, QN * (n % 8):QN * (n % 8) + QN], x[:, t, QN * b:QN * b + QN], ACT.Square,
                       accum_out=x1_parts[:, t, b:b + 1]).then_inc(x1sq, 1)
            inv_rms(x1sum, 1, slice(0, NT), slice(0, NT), D)
            for s, (_, t, q) in enumerate(H2_STEPS):
                act.wait_ge(h2T_ps, s + 1)
                cp(hT[:, 4 * q:4 * q + 4, t * P:(t + 1) * P], bank[s % 2][:, :].rearrange("p (k c) -> p k c", k=4)).then_inc(h2T_sb, 1)
            for t in range(NT):
                act.wait_ge(g_arg, t + 1)
                af(rt[:, t, 128:134], rt[:, t, 128:134], ACT.Exp).then_inc(g_exp, 1)
            for n in range(8):
                act.wait_ge(gbc_ps, 8 + n + 1)
                cp(gbc[:, n // 4, (n % 4) * QN:(n % 4 + 1) * QN], bank[GATE_BANKS[1][n % 4]][:, :]).then_inc(gbc_sb, 1)

            def rows_copy(u, n):
                act.wait_ge(eT_ps, n + 1)
                cp(xeT[u][:, 4:8, :, :].rearrange("p c q s -> p (c q s)"), bank[1][:, :]).then_inc(eT_a, 1)

            def exp_gate(u, e):
                act.wait_ge(gu_ps_need(e)[0], gu_ps_need(e)[1])
                af(sg[u], bank[2 + u][:, 0:256], ACT.Exp, scale=-1.0).then_inc(gu_exp, 1)

            def gu_ps_need(e):
                return unit_used, U_MOE + 8 + e * UE

            def y_copy(u, e, sct_need):
                act.wait_ge(hT_ps, e + 1)
                cp(hidT[u].rearrange("p c q s -> p (c q s)"), bank[4][:, 0:256]).then_inc(hT_sb, 1)
                act.wait_ge(unit_used, U_MOE + UE + e * UE)
                wait_count(act, sct[u], sct_need)
                cp(ysb[u][:, QN:2 * QN], bank[6][:, :]).then_inc(y_a, 1)

            for t in range(NT):
                act.wait_ge(h2_out[t], 16)
            rows_copy(0, 0)

            def two_experts(i):
                for u in range(2):
                    e = 2 * i + u
                    exp_gate(u, e)
                    rows_copy(1 - u, e + 1)
                    y_copy(u, e, 16 * i)

            peeled(act, two_experts, NE // 2)
            act.wait_ge(ov_rdy, 1)
            n_over = act.value_load(ov_i[0:1, 0:1], min_val=0, max_val=NOVER)
            with act.If(n_over > 0):
                with act.Fori(0, n_over) as i:
                    rows_copy(0, i + NE + 1)
                    exp_gate(0, i + NE)
                    y_copy(0, i + NE, 16 * 16 + 16 * i)
            with act.Else():
                act.nop()
            act.wait_ge(moe_done, 1)
            for t in range(NT):
                nc.scalar.dma_start(yk[t], y_rows[t]).then_inc(yk_in[t], 16)

            def gated(t):
                act.wait_ge(yk_in[t], 16)
                af(yk[t][:, 0, :], yk[t][:, 0, :], ACT.Copy, scale=gate[:, 0, t:t + 1]).then_inc(y_gated, 1)

            gated(0)
            gated(1)
            for t in range(NT):
                act.wait_ge(fin_sum, t + 1)
                if t:
                    act.wait_ge(fin_sq, t)
                af(sqf, x[:, t, :], ACT.Square, accum_out=stat[:, t:t + 1]).then_inc(fin_sq, 1)
                inv_rms(fin_sq, t + 1, slice(t, t + 1), slice(t, t + 1), D)
                if t == 0:
                    gated(2)
                if t < 2:
                    act.wait_ge(fin_rs, t + 1)
                    af(x[:, t, :], x[:, t, :], ACT.Copy, scale=rs[:, 0, t:t + 1]).then_inc(fin_rdy, 1)

        @block.vector
        def _(dve):
            link = Chain(dve, ch_v)
            v = nc.vector
            ts, tt, stt, cp = v.tensor_scalar, v.tensor_tensor, v.scalar_tensor_tensor, v.tensor_copy
            link(v.memset(cT, 0.0))
            v.memset(abT, 1.0)
            v.memset(wgate, 0.0).then_inc(gate_zero, 1)
            def refine(done, cols, out, n):
                y, m, w = (rs[:, q, out] for q in range(3))
                dve.wait_ge(rstd, done)
                link_(ts(m, stat[:, cols], 1.0 / n, EPS, ALU.mult, ALU.add))
                link_(tt(w, y, y, ALU.mult))
                link_(tt(w, w, m, ALU.mult))
                link_(ts(w, w, -0.5, 1.5, ALU.mult, ALU.add))
                link_(tt(y, y, w, ALU.mult))

            link_ = Chain(dve, ch_r)
            dve.wait_ge(c_exp, 1)
            link(ts(ctmp, ctmp, 1.0, None, ALU.add))
            link(v.reciprocal(ctmp, ctmp))
            tt(cT[:, :, 0:9], bank[5][:, 0:9 * KC].rearrange("p (k r) -> p k r", k=KC), ctmp, ALU.mult).then_inc(cT_sb, 1)
            refine(1, slice(0, NT), slice(0, NT), D)
            for t in range(NT):
                ts(x[:, t, :], x[:, t, :], rs[:, 0, t:t + 1], None, ALU.mult).then_inc(xn, 1)
            dve.wait_ge(consts, 1)
            dve.wait_ge(bias_in, 16 * 12)
            dve.wait_ge(unit_used, KC)
            tt(modr[:, 0, :], bank[4][:, :], bias[:, 0, :], ALU.add).then_inc(mods, 1)
            dve.wait_ge(unit_used, 2 * KC)
            tt(modr[:, 1, :], bank[5][:, :], bias[:, 1, :], ALU.add).then_inc(mods, 1)
            dve.wait_ge(mods, 2)
            stt(modr[:, 1, :], modr[:, 1, :], 1.0, mix_gain, ALU.add, ALU.mult).then_inc(mods, 1)
            for m in range(2):
                dve.wait_ge(modT_ps, m + 1)
                src = bank[6 + m][:, :].rearrange("p (c g r) -> p g c r", c=4, g=4)[:, :, :, 0:9]
                cp(modT[:, m, :, :].rearrange("p (g c) r -> p g c r", g=4), src).then_inc(modT_sb, 1)
            dve.wait_ge(modT_sb, 2)
            dve.wait_ge(xT_sb, 12)
            for q in range(4):
                hs = hT[:, 4 * q:4 * q + 4, 256:384].rearrange("p k (b n) -> p k b n", b=DEC_B)
                for m, op in ((1, ALU.mult), (0, ALU.add)):
                    c = modT[:, m, 4 * q:4 * q + 4, 1:9].unsqueeze(3).broadcast_to([P, 4, DEC_B, DEC_T])
                    tt(hs, hs, c, op).then_inc(h_sample, 1)
                    if m == 1:
                        dve.wait_ge(h_sample, 2 * q + 1)
            dve.wait_ge(unit_used, U_KVA + 3)
            cp(kva[:, 2, :], bank[2][:, 0:256])
            for q in range(4):
                last = cp(abT[32 * q:32 * q + 16, :], bank[3][32 * q:32 * q + 16, 0:TOK])
            last.then_inc(ev_v, 1)

            with dve.Fori(0, 2) as a:
                for b in range(2):
                    dve.wait_ge(unit_used, 24 * a + (U_T + 12 * b + 4))
                    for c in range(2, 4):
                        last = cp(zT[:, bass.ds(8 * a + (4 * b + c), 1), :].rearrange("p a n -> p (a n)"), bank[c][:, 0:TOK])
                    last.then_inc(ev_v, 1)
                dve.wait_ge(unit_used, 24 * a + (U_T + 24))
                m = bass.ds(a + 2, 1)
                tt(modr[:, m, :].rearrange("p m c -> p (m c)"), bank[4][:, :],
                   bias[:, m, :].rearrange("p m c -> p (m c)"), ALU.add).then_inc(mods, 1)
            vflat = xbuf[:, :].rearrange("p (a c) -> p a c", a=2)
            with dve.Fori(0, 2) as a:
                for b in range(2):
                    dve.wait_ge(unit_used, 8 * a + (U_V + 4 * b + 4))
                    cp(vflat[:, bass.ds(a, 1), 2048 + QN * b:2048 + QN * b + QN].rearrange("p a n -> p (a n)"), bank[2][:, :]).then_inc(ev_v, 1)
            dve.wait_ge(ev_a, 1)
            for u in range(2):
                last = cp(kdup[:, :, :, u, :], kva[:, :, 0:128].rearrange("p t (j c) -> p t j c", j=SWA_KV))
            last.then_inc(kdup_sb, 1)
            dve.wait_ge(unit_used, U_ADA4)
            for j in range(SWA_KV):
                for b in range(DEC_B):
                    cp(q_s[:, b, j, :].rearrange("p (h n) -> p h n", h=4), zT[:, 4 * j:4 * j + 4, 256 + 16 * b:272 + 16 * b])
            dve.wait_ge(kT_ps, 1)
            for j in range(SWA_KV):
                last = cp(kT2[:, j, :], bank[j][:, 0:TOK])
            dve.wait_ge(ch_a, 1)
            link(last)
            cp(stat[:, 42:43], stat[:, 0:1]).then_inc(kT_sb, 1)
            dve.wait_ge(small_in, 16 * 15)

            def soft_a(s):
                st = stat[:, 8 + 8 * (s % 2):16 + 8 * (s % 2)]
                dve.wait_ge(sc_ps, s + 1)
                if s >= 3:
                    dve.wait_ge(pT_ps, s - 2)
                if s < 16:
                    t, m = s // 8, s % 8
                    n = P * (t + 1)
                    sink = sinkb[:, 2 * m:2 * m + 2]
                    for u in range(2):
                        last = stt(sS[s % 3][:, u * n:(u + 1) * n], bank[2 * (s % 2) + u][:, 0:n], HD ** -0.5,
                                   band[:, 256 - n:256], ALU.mult, ALU.add)
                else:
                    n = 144
                    sink = sinks_s[:, :]
                    for u in range(2):
                        r = slice(64 * u, 64 * u + 64)
                        last = ts(sS[s % 3][r, 0:2 * n], bank[2 * (s % 2) + u][r, 0:2 * n], HD ** -0.5, None, ALU.mult)
                last.then_inc(sc_sb, 1)
                dve.wait_ge(sc_sb, s + 1)
                link(v.tensor_reduce(st[:, 6:8], sS[s % 3][:, 0:2 * n].rearrange("p (u n) -> p u n", u=2), AX.X, ALU.max))
                link(tt(st[:, 6:8], st[:, 6:8], sink, ALU.max))
                link(ts(st[:, 0:2], st[:, 6:8], -1.0, None, ALU.mult))
                tt(st[:, 2:4], st[:, 0:2], sink, ALU.add).then_inc(nm_sb, 1)

            def soft_b(s):
                st = stat[:, 8 + 8 * (s % 2):16 + 8 * (s % 2)]
                n = (P * (s // 8 + 1)) if s < 16 else 144
                dve.wait_ge(p_exp, s + 1)
                link(tt(st[:, 4:6], st[:, 4:6], st[:, 2:4], ALU.add))
                link(v.reciprocal(st[:, 4:6], st[:, 4:6]))
                for u in range(2):
                    p = sS[s % 3][:, u * n:(u + 1) * n]
                    last = ts(p, p, st[:, 4 + u:5 + u], None, ALU.mult)
                last.then_inc(p_sb, 1)

            def late_mod(m):
                dve.wait_ge(unit_used, U_ADA4 + KC * (m - 3))
                tt(modr[:, m, :], bank[7][:, :], modr[:, m, :], ALU.add).then_inc(mods, 1)

            for s in range(25):
                if s == 13:
                    late_mod(4)
                if s < 24:
                    soft_a(s)
                if s:
                    soft_b(s - 1)
            late_mod(5)
            dve.wait_ge(o_sb, 24)
            link(v.memset(Sp[0], 0.0))

            def gate_abs(t):
                dve.wait_ge(lg_ps, t + 1)
                link(cp(AT, bank[2][:, :]))
                stt(lg, AT, -1.0, AT, ALU.mult, ALU.max).then_inc(lg_abs, 1)

            def log_sigmoid(t):
                dve.wait_ge(lg_ln, t + 1)
                stt(lg, AT, 0.0, lg, ALU.min, ALU.subtract).then_inc(lg_sb, 1)

            gate_abs(0)
            log_sigmoid(0)
            for t in range(NT):
                cols = slice(t * P, (t + 1) * P)
                dve.wait_ge(cum_exp, t + 1)
                for u in range(2):
                    stt(kk[:, u, :], bank[3][:, :], par_col[:, u:u + 1], esuf, ALU.mult, ALU.mult)
                q3 = zT[:, 8:12, cols]
                k3 = zT[:, 12:16, cols]
                e3 = ebT.rearrange("p (h n) -> p h n", h=GH)
                tt(k3, k3, enbT.rearrange("p (h n) -> p h n", h=GH), ALU.mult)
                link(stt(q3, q3, DK ** -0.5, e3, ALU.mult, ALU.mult))
                for u in range(2):
                    tt(qdm[:, u, :, :], q3, par_row[:, u:u + 1, :].broadcast_to([P, GH, P]), ALU.mult)
                cp(dec[:, :, 8 * t:8 * t + 8], ebT.rearrange("p (h b n) -> p h b n", h=GH, b=8)[:, :, :, 15]).then_inc(qk_sb, 1)
                dve.wait_ge(a_ps, t + 1)
                tt(AT.rearrange("p (h n) -> p h n", h=GH), bank[0][:, :].rearrange("p (h n) -> p h n", h=GH),
                   tri_le[:, :].unsqueeze(1).broadcast_to([P, GH, P]), ALU.mult).then_inc(a_sb, 1)
                for i in range(8):
                    B = 8 * t + i
                    dve.wait_ge(kv_ps, B + 1)
                    if t < 2:
                        S, new = Sp[B % 2], Sp[1 - B % 2]
                        if B:
                            dve.wait_ge(inter, B)
                            dve.wait_ge(s_new, B)
                    else:
                        S, new = Sin[i % 2], Sout[i % 2]
                        dve.wait_ge(s_in[i % 2], 16 * (i // 2 + 1))
                        if i >= 2:
                            dve.wait_ge(s_st[i % 2], 16 * (i // 2))
                        elif i == 1:
                            dve.wait_ge(sp_out, 16)
                    for h in range(GH):
                        c = slice(h * DV, (h + 1) * DV)
                        last = stt(new[:, c], S[:, c], dec[:, h, B:B + 1], bank[kv_bank(i, h)][:, (h % 2) * DV:(h % 2 + 1) * DV],
                                   ALU.mult, ALU.add)
                    last.then_inc(s_new, 1)
                    if i == 0:
                        dve.wait_ge(r_exp, t + 1)
                        link(ts(silu_r, silu_r, 1.0, None, ALU.add))
                    elif i < 5:
                        c = slice((i - 1) * DV, i * DV)
                        link(v.reciprocal(silu_r[:, c], silu_r[:, c]))
                    elif i == 5:
                        link(tt(silu_r, silu_r, vr[:, 1, t, :], ALU.mult))
                    elif i == 6:
                        r4 = silu_r.rearrange("p (h n) -> p h n", h=GH)
                        link(tt(r4, r4, gheadb[:, :].unsqueeze(1).broadcast_to([P, GH, DV]), ALU.mult))
                if t + 1 < NT:
                    gate_abs(t + 1)
                    log_sigmoid(t + 1)
                dve.wait_ge(osq, t + 1)
                refine(t + 2, slice(48, 52), slice(0, 4), DV)
                if t:
                    dve.wait_ge(ogT_ps, 2 * t)
                for h in range(GH):
                    c = slice(h * DV, (h + 1) * DV)
                    last = stt(og[:, c], bank[4 + h][:, 0:DV], rs[:, 0, h:h + 1], silu_r[:, c], ALU.mult, ALU.mult)
                last.then_inc(og_sb, 1)
            dve.wait_ge(router_in, 128)
            dve.wait_ge(mods, NMOD + 1)
            stt(modr[:, 4, :], modr[:, 4, :], 1.0, ffn_gain, ALU.add, ALU.mult).then_inc(mods, 1)
            dve.wait_ge(gbc_sb, 8)
            dve.wait_ge(x_in2, 48)
            dve.nop().then_inc(x1, 1)
            with dve.Fori(0, 2) as a:
                link.enter(a, 6)
                for b in range(2):
                    dve.wait_ge(unit_used, 8 * a + (U_OUT + 4 * b + 4))
                    dve.wait_ge(x1, 2 * a + (b + 1))
                    for t in range(NT):
                        g_ = gbc[:, t // 2, bass.ds(1024 * a + QN * b, QN)]
                        xs = x[:, t, bass.ds(1024 * a + QN * b, QN)]
                        link(tt(mul_tmp[:, t, :], bank[3 * b + t][:, :], g_, ALU.mult))
                        last = tt(xs, xs, mul_tmp[:, t, :], ALU.add)
                    last.then_inc(x1, 1)
                link.leave(2)
            dve.wait_ge(x1sq, 4 * NT)
            v.tensor_reduce(stat[:, 0:NT], x1_parts, AX.X, ALU.add).then_inc(x1sum, 1)
            refine(5, slice(0, NT), slice(0, NT), D)
            for s, (n, t, q) in enumerate(H2_STEPS):
                if s == 8:
                    dve.wait_ge(h2_out[0], 16)
                    dve.wait_ge(h2T_ps, 7)
                c = slice(q * QN, (q + 1) * QN)
                b = 6 - 3 * (n % 2)
                dve.wait_ge(bc_ps, n + 1)
                link(stt(h2[t % 2][:, c], x[:, t, c], rs[:, 0, t:t + 1], bank[b][:, :], ALU.mult, ALU.mult))
                tt(h2[t % 2][:, c], h2[t % 2][:, c], bank[b + 1][:, :], ALU.add).then_inc(h2_v, 1)
            dve.wait_ge(router_in, 128)
            for t in range(NT):
                R = rt[:, t, :]
                dve.wait_ge(logit_ps, t + 1)
                v.memset(R[:, 4:8], -3e38)
                tt(R[:, 0:4], bank[LOGIT_BANK[t]][:, 64 * t:64 * t + 4], br[:, 0:4], ALU.add)
                link(tt(R[:, 8:40], bank[LOGIT_BANK[t]][:, 64 * t + 4:64 * t + 36], br[:, 4:36], ALU.add))
                link(v.max(R[:, 40:48], R[:, 0:8]))
                link(v.max_index(R[:, 48:56].bitcast(U32), R[:, 40:48], R[:, 0:8]))
                link(cp(R[:, 56:57], R[:, 48:49].bitcast(U32)))
                link(ts(R[:, 60:64], iota_e[:, 0:4], R[:, 56:57], None, ALU.is_equal))
                link(ts(R[:, 64:72], R[:, 8:16], R[:, 60:61], None, ALU.mult))
                for q in range(1, 4):
                    link(stt(R[:, 64:72], R[:, 8 + 8 * q:16 + 8 * q], R[:, 60 + q:61 + q], R[:, 64:72], ALU.mult, ALU.add))
                link(v.max(R[:, 72:80], R[:, 64:72]))
                link(v.max_index(R[:, 80:88].bitcast(U32), R[:, 72:80], R[:, 64:72]))
                link(cp(R[:, 88:90], R[:, 80:82].bitcast(U32)))
                link(ts(R[:, 92:93], R[:, 56:57], float(EPG), None, ALU.mult))
                link(ts(R[:, 88:90], R[:, 88:90], R[:, 92:93], None, ALU.add))
                tt(R[:, 132:133], R[:, 73:74], R[:, 72:73], ALU.subtract)
                v.memset(R[:, 133:134], 0.0)
                link(ts(R[:, 128:132], R[:, 0:4], R[:, 40:41], None, ALU.subtract))
                for q in range(2):
                    last = ts(R[:, 160 + 32 * q:192 + 32 * q], iota_e[:, :], R[:, 88 + q:89 + q], None, ALU.is_equal)
                link(last)
                tt(R[:, 96:128], R[:, 160:192], R[:, 192:224], ALU.add).then_inc(rank_rdy, 1)
                v.memset(R[:, 134:136], 0.0).then_inc(g_arg, 1)
            dve.wait_ge(rank_ps, 1)
            picks = rt[:, :, 160:224].rearrange("p t (q e) -> p t q e", q=2)
            ranks = bank[5][:, 0:NT * NE].rearrange("p (t e) -> p t e", t=NT).unsqueeze(2).broadcast_to([P, NT, 2, NE])
            link(tt(picks, picks, ranks, ALU.mult))
            link(v.tensor_reduce(rt[:, :, 140:142], picks, AX.X, ALU.add))
            link(stt(rt[:, :, 142:144], rt[:, :, 88:90], float(TOK), rt[:, :, 140:142], ALU.mult, ALU.add))
            link(cp(dest_i[:, :].rearrange("p (q t) -> p t q", q=2), rt[:, :, 142:144]))
            cp(stat[:, 43:44], stat[:, 0:1]).then_inc(dest_rdy, 1)
            dve.wait_ge(g_exp, NT)
            group_sum, pair_sum, second = rt[:, :, 136], rt[:, :, 137], rt[:, :, 132]
            link(v.tensor_reduce(group_sum, rt[:, :, 128:132], AX.X, ALU.add))
            link(ts(pair_sum, second, 1.0, None, ALU.add))
            link(tt(group_sum, group_sum, pair_sum, ALU.mult))
            link(v.reciprocal(gate[:, 0, :], group_sum))
            link(tt(gate[:, 1, :], gate[:, 0, :], second, ALU.mult))
            cnt = bank[5][0:1, 3 * NE:4 * NE]
            ex, cum, tmp = ov_f[:, 0:32], ov_f[:, 32:64], ov_f[:, 64:96]
            link(v.memset(ex, 0.0))
            for w in range(1, TOK // W):
                link(stt(ex, cnt, float(w * W), ex, ALU.is_gt, ALU.add))
            link(cp(cum, ex))
            for sft in (1, 2, 4, 8, 16):
                link(cp(tmp, cum))
                link(tt(cum[:, sft:32], cum[:, sft:32], tmp[:, 0:32 - sft], ALU.add))
            le = ov_f[:, 128:128 + NOVER * 32].rearrange("p (i e) -> p i e", i=NOVER)
            idx = ov_f[:, 96:96 + NOVER]
            c3 = cum.unsqueeze(1).broadcast_to([1, NOVER, NE])
            i3 = iota_e[0:1, 0:NOVER].unsqueeze(2).broadcast_to([1, NOVER, NE])
            link(tt(le, c3, i3, ALU.is_le))
            res = ov_f[:, 960:1020]
            link(v.tensor_reduce(idx, le, AX.X, ALU.add))
            link(ts(res[:, 1:1 + NOVER], idx, float(NE - 1), None, ALU.min))
            link(tt(le, le, ex.unsqueeze(1).broadcast_to([1, NOVER, NE]), ALU.mult))
            link(v.tensor_reduce(res[:, 1 + NOVER:1 + 2 * NOVER], le, AX.X, ALU.add))
            o = res[:, 1 + NOVER:1 + 2 * NOVER]
            link(tt(o, iota_e[0:1, 0:NOVER], o, ALU.subtract))
            link(ts(o, o, 1.0, float(W), ALU.add, ALU.mult))
            link(stt(o, res[:, 1:1 + NOVER], float(TOK), o, ALU.mult, ALU.add))
            link(cp(res[:, 0:1], cum[:, 31:32]))
            link(cp(ov_i[:, 0:1 + 2 * NOVER], res[:, 0:1 + 2 * NOVER]))
            cp(ov_i[:, 60:61], ov_i[:, 0:1]).then_inc(ov_rdy, 1)
            dve.wait_ge(slots_in, 32)
            f0, f1, f2 = (tab_f[:, q, :] for q in range(3))
            link(cp(f0, tab_a[:, :]))
            link(ts(f1, f0, float(TOK), -float(TOK), ALU.is_ge, ALU.mult))
            link(tt(f1, f1, f0, ALU.add))
            link(ts(f1, f1, 2.0, half[:, 0:1], ALU.mult, ALU.add))
            link(ts(f2, f0, 2.0, half[:, 0:1], ALU.mult, ALU.add))
            cp(gtab[:, 0:NE], f1)
            cp(gtab[:, NE:NE + 1], f1[:, NE - 1:NE])
            link(cp(stab[:, :], f2))
            cp(stat[:, 44:45], stat[:, 0:1]).then_inc(tabs, 1)

            def rows_copy(u, n):
                dve.wait_ge(eT_ps, n + 1)
                cp(xeT[u][:, 0:4, :, :].rearrange("p c q s -> p (c q s)"), bank[0][:, :]).then_inc(eT_v, 1)

            def hidden(u, e):
                dve.wait_ge(gu_exp, e + 1)
                link(ts(sg[u], sg[u], 1.0, None, ALU.add))
                link(v.reciprocal(sg[u], sg[u]))
                link(tt(sg[u], sg[u], bank[2 + u][:, 0:256], ALU.mult))
                tt(hid[u], sg[u], bank[2 + u][:, 256:512], ALU.mult).then_inc(hid_sb, 1)

            def y_copy(u, e, sct_need):
                dve.wait_ge(unit_used, U_MOE + UE + e * UE)
                wait_count(dve, sct[u], sct_need)
                cp(ysb[u][:, 0:QN], bank[5][:, :]).then_inc(y_v, 1)

            rows_copy(0, 0)

            def two_experts(i):
                for u in range(2):
                    e = 2 * i + u
                    hidden(u, e)
                    rows_copy(1 - u, e + 1)
                    y_copy(u, e, 16 * i)

            peeled(dve, two_experts, NE // 2, link, 6)
            n_over = dve.value_load(ov_i[0:1, 0:1], min_val=0, max_val=NOVER)
            with dve.If(n_over > 0):
                with dve.Fori(0, n_over) as i:
                    link.enter(i, 8)
                    dve.wait_ge(ocur_in, 32 * i + 32)
                    a0, m0 = ocur[:, 0, :], ocur[:, 1, :]
                    link(cp(a0, ocur_i))
                    link(ts(m0, a0, float(TOK), -float(TOK), ALU.is_ge, ALU.mult))
                    link(tt(m0, m0, a0, ALU.add))
                    link(ts(m0, m0, 2.0, half[:, 0:1], ALU.mult, ALU.add))
                    link(ts(a0, a0, 2.0, half[:, 0:1], ALU.mult, ALU.add))
                    cp(gcur[:, 0, :], m0)
                    cp(scur[:, 0, :], a0).then_inc(ocur_rdy, 1)
                    rows_copy(0, i + NE + 1)
                    hidden(0, i + NE)
                    y_copy(0, i + NE, 16 * 16 + 16 * i)
            with dve.Else():
                dve.nop()
            fin = Chain(dve, ev_v)
            fin.n = 9
            dve.wait_ge(gfin_in, 16)

            def normed(t):
                refine(t + 6, slice(t, t + 1), slice(t, t + 1), D)
                if t < 2:
                    dve.nop().then_inc(fin_rs, 1)
                    return
                stt(x[:, t, :], x[:, t, :], rs[:, 0, t:t + 1], gfin, ALU.mult, ALU.mult).then_inc(fin_rdy, 1)

            for t in range(NT):
                y0, y1 = yk[t][:, 0, :], yk[t][:, 1, :]
                dve.wait_ge(y_gated, t + 1)
                fin(stt(y0, y1, gate[:, 1, t:t + 1], y0, ALU.mult, ALU.add))
                fin(tt(y0, y0, gbc[:, t // 2, :], ALU.mult))
                tt(x[:, t, :], x[:, t, :], y0, ALU.add).then_inc(fin_sum, 1)
                if t:
                    normed(t - 1)
            normed(NT - 1)


_INS = ["x_prompt", "x_sample", "cache_swa_k", "cache_swa_v", "state_gla", "c_prompt", "c_sample", "g_mix_norm",
        "g_ffn_norm", "w_ada", "b_ada", "w_in", "attn_sinks", "w_gla_gate", "b_gla_gate", "g_gla_norm", "w_out",
        "w_router_group", "b_router_group", "w_router_expert", "b_router_expert", "w_expert_gate", "w_expert_up",
        "w_expert_down", "g_final"]
_OUTS = [("y_prompt", (1, 256, 2048)), ("y_sample", (8, 16, 2048)), ("swa_k_prompt", (1, 1, 128, 2, 64)),
         ("swa_v_prompt", (1, 1, 128, 2, 64)), ("gla_state_prompt", (1, 1, 4, 128, 256)),
         ("swa_k_sample", (1, 8, 16, 2, 64)), ("swa_v_sample", (1, 8, 16, 2, 64)),
         ("gla_state_sample", (1, 8, 4, 128, 256))]


def kernel(**inputs):
    import numpy as _np
    import concourse.bacc as _bacc
    from concourse import mybir as _mybir
    from concourse.bass_utils import run_bass_kernel_spmd as _run

    nc = _bacc.Bacc("TRN2", target_bir_lowering=False, num_devices=1)
    arrays, ins, outs = {}, {}, {}
    for name in _INS:
        a = _np.ascontiguousarray(inputs[name])
        arrays[f"in_{name}"] = a
        ins[name] = nc.dram_tensor(f"in_{name}", a.shape, _mybir.dt.from_np(a.dtype), kind="ExternalInput").ap()
    for name, shape in _OUTS:
        outs[name] = nc.dram_tensor(f"out_{name}", shape, _mybir.dt.float32, kind="ExternalOutput").ap()
    encoder_step(nc, ins, outs)
    r = _run(nc, [arrays], core_ids=[0])
    return tuple(r.results[0][f"out_{name}"] for name, _ in _OUTS)
```
